# Optimizing a Trainium2 kernel written in Bass

```python
import jax, jax.numpy as jnp
from jax import lax
import numpy as np

D_MODEL = 1024
BATCH = 1
SEQ = 512
DEPTH = 1

F32 = jnp.float32
EPS = 1e-6
MEM_LEN = 256
GRID_W = 64
CONV_W = 3
ML_HEADS = 4
ML_HEAD_DIM = 128
ML_WIDTH = ML_HEADS * ML_HEAD_DIM
ML_CHUNK = 64
NA_HEADS = 8
NA_HEAD_DIM = 64
NA_WIDTH = NA_HEADS * NA_HEAD_DIM
NA_WIN_ROWS_MAX = 8
NA_WIN_COLS = 16
XA_HEADS = 4
XA_HEAD_DIM = 128
XA_WIDTH = XA_HEADS * XA_HEAD_DIM
N_BRANCHES = 3
D_FF = 2816
IN_SPLITS = (ML_WIDTH, ML_WIDTH, ML_WIDTH, ML_WIDTH, 4 * ML_HEADS, 3 * NA_WIDTH, XA_WIDTH, N_BRANCHES * D_MODEL)
IN_WIDTH = sum(IN_SPLITS)
NEG_INIT = -1e30


def rms_norm(x, g):
    xf = x.astype(F32)
    y = xf * lax.rsqrt(jnp.mean(xf * xf, axis=-1, keepdims=True) + EPS)
    return (y * g.astype(F32)).astype(x.dtype)

def dwconv3(x, w, b):
    xp = jnp.pad(x, ((0, 0), (1, 1), (0, 0)))
    return xp[:, :-2] * w[0] + xp[:, 1:-1] * w[1] + xp[:, 2:] * w[2] + b

def mlstm_chunkwise(q, k, v, i_pre, f_pre):
    B, H, S, Dh = q.shape
    L = ML_CHUNK
    NC = S // L
    q = q.astype(F32).reshape(B, H, NC, L, Dh) * (Dh ** -0.5)
    k = k.astype(F32).reshape(B, H, NC, L, Dh)
    v = v.astype(F32).reshape(B, H, NC, L, Dh)
    log_f = jax.nn.log_sigmoid(f_pre.astype(F32)).reshape(B, H, NC, L)
    log_i = i_pre.astype(F32).reshape(B, H, NC, L)
    a = jnp.cumsum(log_f, axis=-1)
    g = a[..., -1]
    w_end = g[..., None] - a + log_i
    m_end = jnp.max(w_end, axis=-1)

    def step(carry, xs):
        C, n, m = carry
        k_c, v_c, w_c, mw_c, g_c = xs
        m_new = jnp.maximum(g_c + m, mw_c)
        decay = jnp.exp(g_c + m - m_new)
        wt = jnp.exp(w_c - m_new[..., None])
        C_new = decay[..., None, None] * C + jnp.einsum('bhl,bhld,bhle->bhde', wt, v_c, k_c)
        n_new = decay[..., None] * n + jnp.einsum('bhl,bhle->bhe', wt, k_c)
        return (C_new, n_new, m_new), (C, n, m)

    init = (jnp.zeros((B, H, Dh, Dh), F32), jnp.zeros((B, H, Dh), F32), jnp.full((B, H), NEG_INIT, F32))
    xs = (jnp.moveaxis(k, 2, 0), jnp.moveaxis(v, 2, 0), jnp.moveaxis(w_end, 2, 0),
          jnp.moveaxis(m_end, 2, 0), jnp.moveaxis(g, 2, 0))
    _, (C_prev, n_prev, m_prev) = lax.scan(step, init, xs)
    C_prev = jnp.moveaxis(C_prev, 0, 2)
    n_prev = jnp.moveaxis(n_prev, 0, 2)
    m_prev = jnp.moveaxis(m_prev, 0, 2)

    causal = jnp.tril(jnp.ones((L, L), dtype=bool))
    D = a[..., :, None] - a[..., None, :] + log_i[..., None, :]
    D = jnp.where(causal, D, -jnp.inf)
    inter_log = a + m_prev[..., None]
    m_j = jnp.maximum(inter_log, jnp.max(D, axis=-1))
    qk = jnp.einsum('bhcjd,bhcsd->bhcjs', q, k)
    P = jnp.exp(D - m_j[..., None]) * qk
    inter_w = jnp.exp(inter_log - m_j)
    num = jnp.einsum('bhcjs,bhcsd->bhcjd', P, v) + inter_w[..., None] * jnp.einsum('bhcde,bhcje->bhcjd', C_prev, q)
    den = jnp.sum(P, axis=-1) + inter_w * jnp.einsum('bhce,bhcje->bhcj', n_prev, q)
    h = num / jnp.maximum(jnp.abs(den), jnp.exp(-m_j))[..., None]
    return h.reshape(B, H, S, Dh)

def mlstm_branch(q_pre, k_pre, v, o_pre, gates, w_conv, b_conv, b_ig, b_fg, norm_g):
    B, S, _ = q_pre.shape
    qk = jax.nn.silu(dwconv3(jnp.concatenate([q_pre, k_pre], axis=-1), w_conv, b_conv))
    q, k = jnp.split(qk, 2, axis=-1)
    heads = lambda t: t.reshape(B, S, ML_HEADS, ML_HEAD_DIM).transpose(0, 2, 1, 3)
    qh, kh, vh = heads(q), heads(k), heads(v)
    gt = gates.astype(F32).reshape(B, S, 4, ML_HEADS).transpose(2, 0, 3, 1)
    b_ig = b_ig.astype(F32)
    b_fg = b_fg.astype(F32)
    i_fw = gt[0] + b_ig[0][None, :, None]
    f_fw = gt[1] + b_fg[0][None, :, None]
    i_bw = gt[2] + b_ig[1][None, :, None]
    f_bw = gt[3] + b_fg[1][None, :, None]
    h_fw = mlstm_chunkwise(qh, kh, vh, i_fw, f_fw)
    flip = lambda t: jnp.flip(t, axis=2)
    h_bw = flip(mlstm_chunkwise(flip(qh), flip(kh), flip(vh), flip(i_bw), flip(f_bw)))
    h = h_fw + h_bw
    h = h * lax.rsqrt(jnp.mean(h * h, axis=-1, keepdims=True) + EPS)
    h = h * norm_g.astype(F32).reshape(ML_HEADS, 1, ML_HEAD_DIM)
    h = h.transpose(0, 2, 1, 3).reshape(B, S, ML_WIDTH)
    return (jax.nn.sigmoid(o_pre.astype(F32)) * h).astype(q_pre.dtype)

def neighbourhood_attention(q, k, v, rpb):
    B, S, _ = q.shape
    rows = S // GRID_W
    kr = min(NA_WIN_ROWS_MAX, rows)
    grid = lambda t: t.reshape(B, rows, GRID_W, NA_HEADS, NA_HEAD_DIM).transpose(0, 3, 1, 2, 4)
    qg, kg, vg = grid(q).astype(F32), grid(k), grid(v)
    r = jnp.arange(rows)
    row_start = jnp.clip(r - kr // 2, 0, rows - kr)
    row_idx = row_start[:, None] + jnp.arange(kr)[None, :]
    k_band = kg[:, :, row_idx].astype(F32)
    v_band = vg[:, :, row_idx].astype(F32)
    c = jnp.arange(GRID_W)
    col_start = jnp.clip(c - NA_WIN_COLS // 2, 0, GRID_W - NA_WIN_COLS)
    col_ok = (c[None, :] >= col_start[:, None]) & (c[None, :] < col_start[:, None] + NA_WIN_COLS)
    dr = row_idx - r[:, None] + (NA_WIN_ROWS_MAX - 1)
    dc = jnp.clip(c[None, :] - c[:, None] + (NA_WIN_COLS - 1), 0, 2 * NA_WIN_COLS - 2)
    bias = rpb.astype(F32)[:, dr[:, None, :, None], dc[None, :, None, :]]
    s = jnp.einsum('bhrcd,bhrkjd->bhrckj', qg, k_band) * (NA_HEAD_DIM ** -0.5) + bias[None]
    s = jnp.where(col_ok[None, None, None, :, None, :], s, -jnp.inf)
    p = jax.nn.softmax(s.reshape(B, NA_HEADS, rows, GRID_W, kr * GRID_W), axis=-1).reshape(s.shape)
    o = jnp.einsum('bhrckj,bhrkjd->bhrcd', p, v_band)
    return o.transpose(0, 2, 3, 1, 4).reshape(B, S, NA_WIDTH).astype(q.dtype)

def memory_cross_attention(q, mem_k, mem_v):
    B, S, _ = q.shape
    M = mem_k.shape[1]
    qh = q.reshape(B, S, XA_HEADS, XA_HEAD_DIM).astype(F32)
    kh = mem_k.reshape(B, M, XA_HEADS, XA_HEAD_DIM).astype(F32)
    vh = mem_v.reshape(B, M, XA_HEADS, XA_HEAD_DIM).astype(F32)
    s = jnp.einsum('bshd,bmhd->bhsm', qh, kh) * (XA_HEAD_DIM ** -0.5)
    p = jax.nn.softmax(s, axis=-1)
    o = jnp.einsum('bhsm,bmhd->bshd', p, vh)
    return o.reshape(B, S, XA_WIDTH).astype(q.dtype)

def conv_glu_ffn(h, w_up, w_conv, b_conv, w_down):
    a, u = jnp.split(h @ w_up, 2, axis=-1)
    return (jax.nn.gelu(dwconv3(a, w_conv, b_conv)) * u) @ w_down

def first_inputs(seed: int = 0) -> dict:
    key = jax.random.key(seed)
    ks = jax.random.split(key, 24)

    def dense(k, shape, fan_in):
        return jax.random.normal(k, shape, F32) * (fan_in ** -0.5)

    def gain(k, shape):
        return 1.0 + 0.05 * jax.random.normal(k, shape, F32)

    def small(k, shape, scale):
        return scale * jax.random.normal(k, shape, F32)

    L = DEPTH
    return {
        "x": jax.random.normal(ks[0], (BATCH, SEQ, D_MODEL), F32),
        "mem": jax.random.normal(ks[1], (BATCH, MEM_LEN, D_MODEL), F32),
        "mix_norm_g": gain(ks[2], (L, D_MODEL)),
        "w_in": dense(ks[3], (L, D_MODEL, IN_WIDTH), D_MODEL),
        "b_ml_igate": small(ks[4], (L, 2, ML_HEADS), 0.1),
        "b_ml_fgate": jnp.linspace(3.0, 6.0, ML_HEADS, dtype=F32) + small(ks[5], (L, 2, ML_HEADS), 0.1),
        "w_ml_conv": dense(ks[6], (L, CONV_W, 2 * ML_WIDTH), CONV_W),
        "b_ml_conv": small(ks[7], (L, 2 * ML_WIDTH), 0.02),
        "ml_norm_g": gain(ks[8], (L, ML_WIDTH)),
        "na_rpb": small(ks[9], (L, NA_HEADS, 2 * NA_WIN_ROWS_MAX - 1, 2 * NA_WIN_COLS - 1), 0.1),
        "mem_norm_g": gain(ks[10], (L, D_MODEL)),
        "w_mem_kv": dense(ks[11], (L, D_MODEL, 2 * XA_WIDTH), D_MODEL),
        "b_merge_gate": small(ks[12], (L, N_BRANCHES * D_MODEL), 0.02),
        "w_br_ml": dense(ks[13], (L, ML_WIDTH, D_MODEL), ML_WIDTH),
        "w_br_na": dense(ks[14], (L, NA_WIDTH, D_MODEL), NA_WIDTH),
        "w_br_xa": dense(ks[15], (L, XA_WIDTH, D_MODEL), XA_WIDTH),
        "w_out": dense(ks[16], (L, D_MODEL, D_MODEL), D_MODEL),
        "ffn_norm_g": gain(ks[17], (L, D_MODEL)),
        "w_ffn_up": dense(ks[18], (L, D_MODEL, 2 * D_FF), D_MODEL),
        "w_ffn_conv": dense(ks[19], (L, CONV_W, D_FF), CONV_W),
        "b_ffn_conv": small(ks[20], (L, D_FF), 0.02),
        "w_ffn_down": dense(ks[21], (L, D_FF, D_MODEL), D_FF),
        "final_norm_g": gain(ks[22], (D_MODEL,)),
    }

def first_block(x, mem, mix_norm_g, w_in, b_ml_igate, b_ml_fgate, w_ml_conv, b_ml_conv, ml_norm_g,
              na_rpb, mem_norm_g, w_mem_kv, b_merge_gate, w_br_ml, w_br_na, w_br_xa, w_out,
              ffn_norm_g, w_ffn_up, w_ffn_conv, b_ffn_conv, w_ffn_down, final_norm_g):
    split_points = [int(p) for p in np.cumsum(IN_SPLITS)[:-1]]
    for l in range(DEPTH):
        h = rms_norm(x, mix_norm_g[l])
        proj = h @ w_in[l]
        ml_q, ml_k, ml_v, ml_o, ml_gates, na_qkv, xa_q, merge_pre = jnp.split(proj, split_points, axis=-1)
        y_ml = mlstm_branch(ml_q, ml_k, ml_v, ml_o, ml_gates, w_ml_conv[l], b_ml_conv[l],
                            b_ml_igate[l], b_ml_fgate[l], ml_norm_g[l])
        na_q, na_k, na_v = jnp.split(na_qkv, 3, axis=-1)
        y_na = neighbourhood_attention(na_q, na_k, na_v, na_rpb[l])
        mem_k, mem_v = jnp.split(rms_norm(mem, mem_norm_g[l]) @ w_mem_kv[l], 2, axis=-1)
        y_xa = memory_cross_attention(xa_q, mem_k, mem_v)
        gates = jax.nn.sigmoid((merge_pre + b_merge_gate[l]).astype(F32)).astype(x.dtype)
        g_ml, g_na, g_xa = jnp.split(gates, N_BRANCHES, axis=-1)
        merged = g_ml * (y_ml @ w_br_ml[l]) + g_na * (y_na @ w_br_na[l]) + g_xa * (y_xa @ w_br_xa[l])
        x = x + merged @ w_out[l]
        x = x + conv_glu_ffn(rms_norm(x, ffn_norm_g[l]), w_ffn_up[l], w_ffn_conv[l], b_ffn_conv[l], w_ffn_down[l])
    return rms_norm(x, final_norm_g)


DEPTH_2 = 2

N_A = DEPTH_2 // 2
N_B = DEPTH_2 - N_A
N_HEADS = 16
HEAD_DIM = D_MODEL // N_HEADS
Q_BLOCK = 128


def rmsnorm(x, g):
    xf = x.astype(jnp.float32)
    y = xf * lax.rsqrt(jnp.mean(xf * xf, axis=-1, keepdims=True) + EPS)
    return (y * g).astype(x.dtype)

def causal_dwconv(u, w):
    width = w.shape[0]
    s = u.shape[1]
    up = jnp.pad(u, ((0, 0), (width - 1, 0), (0, 0)))
    return sum(up[:, i:i + s] * w[i] for i in range(width))

def short_conv_mixer(xn, w_in, conv_w, w_out):
    proj = xn @ w_in
    b, c, h = jnp.split(proj, 3, axis=-1)
    u = causal_dwconv(c * h, conv_w)
    return (b * u) @ w_out

def conv_ffn(xn, w_up, conv_w, w_down):
    up = xn @ w_up
    a, g = jnp.split(up, 2, axis=-1)
    a = causal_dwconv(a, conv_w)
    return (jax.nn.silu(a) * g) @ w_down

def forgetting_attention(q, k, v, c):
    bsz, nh, s_len, hd = q.shape
    nb = s_len // Q_BLOCK
    scale = hd ** -0.5
    qb = q.reshape(bsz, nh, nb, Q_BLOCK, hd).transpose(2, 0, 1, 3, 4)
    cb = c.reshape(bsz, nh, nb, Q_BLOCK).transpose(2, 0, 1, 3)
    kpos = jnp.arange(s_len)

    def one_block(args):
        q_i, c_i, i = args
        s = jnp.einsum('bhqd,bhkd->bhqk', q_i, k, preferred_element_type=jnp.float32) * scale
        s = s + c_i[..., None] - c[:, :, None, :]
        qpos = i * Q_BLOCK + jnp.arange(Q_BLOCK)
        s = jnp.where(kpos[None, :] <= qpos[:, None], s, -jnp.inf)
        p = jax.nn.softmax(s, axis=-1)
        return jnp.einsum('bhqk,bhkd->bhqd', p.astype(v.dtype), v)

    o = lax.map(one_block, (qb, cb, jnp.arange(nb)))
    return o.transpose(1, 0, 3, 2, 4).reshape(bsz, s_len, nh * hd)

def second_inputs(seed: int = 0) -> dict:
    key = jax.random.key(seed)
    ks = jax.random.split(key, 17)
    f32 = jnp.float32
    out_scale = (2 * DEPTH_2) ** -0.5

    def nrm(k, shape, scale):
        return jax.random.normal(k, shape, f32) * scale

    def gain(k, shape):
        return 1.0 + 0.02 * jax.random.normal(k, shape, f32)

    x = nrm(ks[0], (BATCH, SEQ, D_MODEL), 1.0)
    attn_norm = gain(ks[1], (DEPTH_2, D_MODEL))
    ffn_norm = gain(ks[2], (DEPTH_2, D_MODEL))
    a_w_in = nrm(ks[3], (N_A, D_MODEL, 3 * D_MODEL), D_MODEL ** -0.5)
    a_conv = nrm(ks[4], (N_A, CONV_W, D_MODEL), CONV_W ** -0.5)
    a_w_out = nrm(ks[5], (N_A, D_MODEL, D_MODEL), out_scale * D_MODEL ** -0.5)
    kv_norm = gain(ks[6], (D_MODEL,))
    w_kvf = jnp.concatenate([
        nrm(ks[7], (D_MODEL, 2 * D_MODEL), D_MODEL ** -0.5),
        nrm(ks[8], (D_MODEL, N_HEADS), 0.1 * D_MODEL ** -0.5),
    ], axis=1)
    b_f = jax.random.uniform(ks[9], (N_HEADS,), f32, 1.0, 6.0)
    k_norm = gain(ks[10], (HEAD_DIM,))
    b_w_qg = nrm(ks[11], (N_B, D_MODEL, 2 * D_MODEL), D_MODEL ** -0.5)
    q_norm = gain(ks[12], (N_B, HEAD_DIM))
    b_w_out = nrm(ks[13], (N_B, D_MODEL, D_MODEL), out_scale * D_MODEL ** -0.5)
    ffn_w_up = nrm(ks[14], (DEPTH_2, D_MODEL, 2 * D_FF), D_MODEL ** -0.5)
    ffn_conv = nrm(ks[15], (DEPTH_2, CONV_W, D_FF), CONV_W ** -0.5)
    ffn_w_down = nrm(ks[16], (DEPTH_2, D_FF, D_MODEL), out_scale * D_FF ** -0.5)
    return {"x": x, "attn_norm": attn_norm, "ffn_norm": ffn_norm,
            "a_w_in": a_w_in, "a_conv": a_conv, "a_w_out": a_w_out,
            "kv_norm": kv_norm, "w_kvf": w_kvf, "b_f": b_f, "k_norm": k_norm,
            "b_w_qg": b_w_qg, "q_norm": q_norm, "b_w_out": b_w_out,
            "ffn_w_up": ffn_w_up, "ffn_conv": ffn_conv, "ffn_w_down": ffn_w_down}

def second_block(x, attn_norm, ffn_norm, a_w_in, a_conv, a_w_out, kv_norm, w_kvf, b_f,
              k_norm, b_w_qg, q_norm, b_w_out, ffn_w_up, ffn_conv, ffn_w_down):
    bsz, s_len, d = x.shape
    k = v = c = None
    for l in range(DEPTH_2):
        if l < N_A:
            xn = rmsnorm(x, attn_norm[l])
            x = x + short_conv_mixer(xn, a_w_in[l], a_conv[l], a_w_out[l])
        else:
            if l == N_A:
                h = rmsnorm(x, kv_norm)
                kvf = h @ w_kvf
                k_s = kvf[..., :d].reshape(bsz, s_len, N_HEADS, HEAD_DIM)
                v_s = kvf[..., d:2 * d].reshape(bsz, s_len, N_HEADS, HEAD_DIM)
                f_logit = (kvf[..., 2 * d:] + b_f).astype(jnp.float32)
                k = rmsnorm(k_s, k_norm).transpose(0, 2, 1, 3)
                v = v_s.transpose(0, 2, 1, 3)
                c = jnp.cumsum(jax.nn.log_sigmoid(f_logit), axis=1).transpose(0, 2, 1)
            j = l - N_A
            xn = rmsnorm(x, attn_norm[l])
            qg = xn @ b_w_qg[j]
            q = rmsnorm(qg[..., :d].reshape(bsz, s_len, N_HEADS, HEAD_DIM), q_norm[j])
            q = q.transpose(0, 2, 1, 3)
            o = forgetting_attention(q, k, v, c)
            o = o * jax.nn.sigmoid(qg[..., d:])
            x = x + o @ b_w_out[j]
        xn = rmsnorm(x, ffn_norm[l])
        x = x + conv_ffn(xn, ffn_w_up[l], ffn_conv[l], ffn_w_down[l])
    return x


def setup_inputs(seed=0):
    out = dict(first_inputs(seed))
    for name, value in second_inputs(seed + 1).items():
        if name != "x":
            out[name + "_2"] = value
    return out


def reference(
    x, mem, mix_norm_g, w_in, b_ml_igate, b_ml_fgate, w_ml_conv, b_ml_conv, ml_norm_g, na_rpb,
    mem_norm_g, w_mem_kv, b_merge_gate, w_br_ml, w_br_na, w_br_xa, w_out, ffn_norm_g, w_ffn_up,
    w_ffn_conv, b_ffn_conv, w_ffn_down, final_norm_g, attn_norm_2, ffn_norm_2, a_w_in_2,
    a_conv_2, a_w_out_2, kv_norm_2, w_kvf_2, b_f_2, k_norm_2, b_w_qg_2, q_norm_2, b_w_out_2,
    ffn_w_up_2, ffn_conv_2, ffn_w_down_2,
):
    x = first_block(
        x, mem, mix_norm_g, w_in, b_ml_igate, b_ml_fgate, w_ml_conv, b_ml_conv, ml_norm_g,
        na_rpb, mem_norm_g, w_mem_kv, b_merge_gate, w_br_ml, w_br_na, w_br_xa, w_out,
        ffn_norm_g, w_ffn_up, w_ffn_conv, b_ffn_conv, w_ffn_down, final_norm_g,
    )
    return second_block(
        x, attn_norm_2, ffn_norm_2, a_w_in_2, a_conv_2, a_w_out_2, kv_norm_2, w_kvf_2, b_f_2,
        k_norm_2, b_w_qg_2, q_norm_2, b_w_out_2, ffn_w_up_2, ffn_conv_2, ffn_w_down_2,
    )


_drawn_inputs = setup_inputs


def setup_inputs(seed=0):
    import zlib

    import numpy as np

    out = dict(_drawn_inputs(seed))
    spreads = {}
    factors = {'b_ml_igate': 8.0,
     'b_ml_conv': 7.156,
     'ml_norm_g': 2.826,
     'na_rpb': 5.397,
     'mem_norm_g': 8.0,
     'b_merge_gate': 8.0,
     'b_ffn_conv': 4.186,
     'attn_norm_2': 3.394,
     'ffn_norm_2': 5.395,
     'kv_norm_2': 28.728,
     'k_norm_2': 32.707,
     'q_norm_2': 27.253}
    for name, (base, spread) in spreads.items():
        noise = np.random.default_rng([zlib.crc32(name.encode()), seed]).standard_normal(out[name].shape)
        drawn = base * np.exp(spread * noise) if base else spread * noise
        out[name] = __import__('jax').numpy.asarray(drawn.astype(out[name].dtype))
    for name, factor in factors.items():
        out[name] = (out[name] * factor).astype(out[name].dtype)
    return out
```

```python
import numpy as np
import concourse.bass as bass
from concourse import mybir

F32 = mybir.dt.float32
F32R = mybir.dt.float32r
ALU = mybir.AluOpType
ACT = mybir.ActivationFunctionType
AX = mybir.AxisListType

P = 128
D = 1024
KB = D // P
S = 512
TB = S // P
M = 256
MB = M // P
F = 2816
FB = F // P
NSLOT = 4
UW = KB * P
EPS = 1e-6
NEG = -1e30
ML_H, XA_H, FA_PAIRS, NA_PAIRS = 4, 4, 8, 4
GRID = 64
RPB_R, RPB_C = 15, 31
RPB_W = GRID - 16 + RPB_C + GRID - 16
DOWN_KC = (8, 7, 7)

_COLS = [("mix_g", KB), ("mem_g", KB), ("mlc0", 8), ("mlc1", 8), ("mlc2", 8), ("mlb", 8), ("mlg", 4),
         ("bmg", 24), ("fg0", KB), ("fc00", FB), ("fc01", FB), ("fc02", FB), ("fb0", FB), ("gb", 1),
         ("ag0", KB), ("ag1", KB), ("fg1", KB), ("fg2", KB), ("ac0", KB), ("ac1", KB), ("ac2", KB), ("kvg", KB),
         ("bf", 1), ("kn", 1), ("qn", 1), ("fc10", FB), ("fc11", FB), ("fc12", FB), ("fc20", FB), ("fc21", FB),
         ("fc22", FB), ("fin", KB)]
COL, NCOL = {}, 0
for _n, _w in _COLS:
    COL[_n] = NCOL
    NCOL += _w

SLOTS = []
for _n in range(4):
    SLOTS.append((("memk", _n), None))
for _n in range(4):
    SLOTS.append((("memv", _n), None))
for _n in range(4):
    SLOTS.append((("xq", _n), None))
for _j, _un in enumerate((("naq", 0), ("nak", 0), ("nav", 0), ("gate", 0), None, None, None, None)):
    SLOTS.append((_un, ("xa", _j // 4, _j % 4)))
for _p in range(3):
    for _s, _un in enumerate((("naq", _p + 1), ("nak", _p + 1), ("nav", _p + 1), None)):
        SLOTS.append((_un, ("na", _p, _s)))
for _s, _un in enumerate(("mlq", "mlk", "mlv", "mlo")):
    SLOTS.append(((_un, 0), ("na", 3, _s)))
for _h in range(3):
    for _s, _un in enumerate(("mlq", "mlk", "mlv", "mlo")):
        SLOTS.append(((_un, _h + 1), ("ml", _h, _s)))
for _q in range(8):
    SLOTS.append((("mg", _q) if _q < 6 else None, ("ml", 3, _q) if _q < 4 else ("end", 4, _q - 4)))
UNITS = [u for u, _ in SLOTS if u is not None]
UIDX = {u: n for n, u in enumerate(UNITS)}
NATT = len(UNITS)
BIAS_AFTER = {("naq", 0): 0, ("naq", 1): 1, ("naq", 3): 2, ("mlq", 0): 3}
STEPS = [s for _, s in SLOTS if s is not None and s[0] in ("xa", "na")]
SIDX = {s: n for n, s in enumerate(STEPS)}
LEV = {}
VEV = {}
PRE, EXTRA = [], []
GATE_T = SLOTS.index((("gate", 0), ("xa", 0, 3)))
_prev = None
for _t, (_un, _st) in enumerate(SLOTS):
    _pre = [("hn", _st[1] - 1)] if _st and _st[0] in ("ml", "end") and _st[1] >= 1 and _st[2] == 3 else []
    _ex = []
    if _prev is not None and _prev[0] in ("memv", "nav", "mlv"):
        _ex.append(("tr",) + _prev)
    if _t == GATE_T + 4:
        _ex.append(("tr", "gate", 0))
    for _e in _pre + ([_un] if _un else []) + _ex:
        LEV[_e] = len(LEV)
        if _e[0] == "tr":
            VEV[_e[1:]] = len(VEV)
    PRE.append(_pre)
    EXTRA.append(_ex)
    _prev = _un
NL1 = len(LEV)

U, O = {}, {}
_u, _o = NATT, NL1
for _n, _nu, _no in (("merge", 42, 42), ("out", 8, 8), ("up0", 44, 44), ("down0", 24, 8), ("ain", 24, 24),
                     ("aout", 8, 8), ("up1", 44, 44), ("down1", 24, 8), ("f", 1, 1), ("fa", 32, 0)):
    U[_n], O[_n] = _u, _o
    _u, _o = _u + _nu, _o + _no
UM, OM = U["merge"] - 6, O["merge"] - 6
FA_L = 7
_o = O["fa"] + FA_L * FA_PAIRS
for _n, _nu, _no in (("bout", 8, 8), ("up2", 44, 44), ("down2", 24, 8)):
    U[_n], O[_n] = _u, _o
    _u, _o = _u + _nu, _o + _no
NUNITS = _u
HALF = ("mlq", "mlk", "mlo", "mg")
SPL = {"mem": 0, "x": 8, "out": 16, "down0": 24, "aout": 32, "down1": 40, "bout": 48}
NORM = {"mem": 0, "x": 1, "out": 2, "down0": 3, "aout": 4, "down1": 5, "bout": 6}


def two_blocks(nc, A, out):
    base = (nc.sbuf_base + 63) // 64 * 64
    top = [base]

    def fixed(name, shape, dt=F32):
        t = nc.alloc_sbuf_tensor_at(name, shape, dt, offset=top[0])
        n = 4
        for d in shape[1:]:
            n *= d
        top[0] += (n + 31) // 32 * 32
        return t

    X = fixed("X", [P, KB, S])
    XH = fixed("XH", [P, KB, S], F32R)
    XL = fixed("XL", [P, KB, S], F32R)
    RAW = fixed("RAW", [P, NSLOT, UW])
    WH = fixed("WH", [P, NSLOT, UW], F32R)
    WL = fixed("WL", [P, NSLOT, UW], F32R)
    R = fixed("R", [P, S])
    RM = fixed("RM", [P, M])
    SS = fixed("SS", [P, S])
    SQ = fixed("SQ", [P, S])
    TA = fixed("TA", [P, S])
    TC = fixed("TC", [P, S])
    TD = fixed("TD", [P, S])
    TE = fixed("TE", [P, S])
    ONES = fixed("ONES", [P, P])
    BLK = fixed("BLK", [P, P])
    IDN = fixed("IDN", [P, P])
    LO = fixed("LO", [P, P])
    UP = fixed("UP", [P, P])
    PAR = fixed("PAR", [P, NCOL])
    HB = fixed("HB", [P, 24])
    UT = fixed("UT", [P, TB, 64])
    EPSC = fixed("EPSC", [P, 2])
    GE = fixed("GE", [P, KB])
    MX = fixed("MX", [P, 2])
    NX = fixed("NX", [P, 2])
    RS = fixed("RS", [P, 2])
    RI = fixed("RI", [P, 2])
    zone = top[0]
    assert zone + 91 * 1024 <= nc.sbuf_usable_end, (zone, nc.sbuf_usable_end)

    def at(name, kib, shape, dt=F32):
        n = 4
        for d in shape[1:]:
            n *= d
        assert kib * 1024 + n <= 91 * 1024
        return nc.alloc_sbuf_tensor_at(name, shape, dt, offset=zone + int(kib * 1024))

    NM = at("NM", 90, [P, 2, P])
    Y = at("Y", 0, [P, 12, S])
    MEMT = at("MEMT", 0, [P, KB, M])
    SX = at("SX", 24, [P, 2, S])
    PT = at("PT", 28, [P, 2, S])
    PB = at("PB", 32, [P, 3, S])
    ZERO = at("ZERO", 32, [P, M])
    GU = at("GU", 34, [64, 2, S])
    Q = at("Q", 38, [P, 2, S])
    K = at("K", 42, [P, 2, S])
    V = at("V", 46, [P, 2, TB, P])
    SO = at("SO", 50, [P, 2, S])
    XQ = at("XQ", 38, [P, 4, S])
    MK = at("MK", 46, [P, 4, M])
    MV = at("MV", 50, [P, MB, 4 * P])
    GT = at("GT", 54, [64, 4, S])
    UE = at("UE", 54, [P, ML_H, 4, S])
    MH = at("MH", 62, [P, KB, M], F32R)
    ML = at("ML", 70, [P, KB, M], F32R)
    QN = at("QN", 62, [P, 2, S])
    KN = at("KN", 66, [P, 2, S])
    VN = at("VN", 70, [P, 2, TB, P])
    BN = at("BN", 74, [P, 2, 2, 14, GRID])
    FI = at("FI", 54, [P, 2, S])
    EG = at("EG", 76, [P, 6, S])
    YH = at("YH", 24, [P, 12, S], F32R)
    YL = at("YL", 48, [P, 12, S], F32R)
    GH = at("GH", 0, [P, KB, S], F32R)
    GL = at("GL", 72, [P, KB, S], F32R)
    FH = at("FH", 0, [P, FB, S], F32R)
    FL = at("FL", 44, [P, FB, S], F32R)
    AH = at("AH", 0, [P, KB, S], F32R)
    AL = at("AL", 16, [P, KB, S], F32R)
    FQ = at("FQ", 32, [P, 2, S])
    FK = at("FK", 36, [P, 2, S])
    FV = at("FV", 40, [P, 2, TB, P])
    FG = at("FG", 44, [P, 2, S])
    FX = at("FX", 48, [P, 2, S])
    FP = at("FP", 52, [P, 2, S])
    CB = at("CB", 56, [P, 2, 2, S])
    FY = at("FY", 64, [P, KB, S])
    FC = at("FC", 80, [16, 3, S])
    NMR = at("NMR", 86, [P, 2, P], F32R)
    IDR = at("IDR", 87, [P, P], F32R)

    UE_AT = (0, 3, 2, 1)
    bank = [nc.alloc_psum_tensor(f"bank{b}", [P, S], F32) for b in range(8)]
    LB = bank[0:2]
    SB = bank[2:4]
    TRB = bank[4:6]
    OB = bank[6:8]
    NB = bank[7]

    gates_d = nc.dram_tensor("gates_scratch", [2, 64, S], F32, kind="Internal").ap()
    fc_d = nc.dram_tensor("forget_scratch", [16, S], F32, kind="Internal").ap()

    sem = nc.alloc_semaphore
    raw_full = [sem(f"raw_full{s}") for s in range(NSLOT)]
    hi_ready, lo_ready, unit_done = sem("hi_ready"), sem("lo_ready"), sem("unit_done")
    lin_free = sem("lin_free")
    par_ready = sem("par_ready")
    x_in, par_in, mem_in, consts, masks = [sem(f"x_in{h}") for h in range(4)], sem("par_in"), sem("mem_in"), sem("consts"), sem("masks")
    sq_ready, split_ready = sem("sq_ready"), sem("split_ready")
    fin_sum = sem("fin_sum")
    norm_sum, r_ready = sem("norm_sum"), sem("r_ready")
    epi_done, half_act, v_src, v_ready = sem("epi_done"), sem("half_act"), sem("v_src"), sem("v_ready")
    extra_full = sem("extra_full")
    s_full, s_read, mx_ready, p_exp, p_ready = (sem(n) for n in ("s_full", "s_read", "mx_ready", "p_exp", "p_ready"))
    t_full, t_out, pv_done, o_free = sem("t_full"), sem("t_out"), sem("pv_done"), sem("o_free")
    bias_in = [sem("bias_in0"), sem("bias_in1")]
    bias_ready = sem("bias_ready")
    gate_dve, gate_act, gates_out, ue_in = sem("gate_dve"), sem("gate_act"), sem("gates_out"), sem("ue_in")
    e_arg, e_ready, ms_full, ms_read, mp_ready, mpv_done, nd_free = (
        sem(n) for n in ("e_arg", "e_ready", "ms_full", "ms_read", "mp_ready", "mpv_done", "nd_free"))
    h_ready, h_sq, h_sum, h_rs, y_arg, y_done = (sem(n) for n in ("h_ready", "h_sq", "h_sum", "h_rs", "y_arg", "y_done"))
    yh_ready, y_ready = sem("yh_ready"), sem("y_ready")
    mg_arg, mg_act, mrg, mrg_hi, mrg_lo = (sem(n) for n in ("mg_arg", "mg_act", "mrg", "mrg_hi", "mrg_lo"))
    conv_ready, glu_ready, ff_ready, ffh_ready, ffl_ready = (
        sem(n) for n in ("conv_ready", "glu_ready", "ff_ready", "ffh_ready", "ffl_ready"))
    a_ready, ah_ready, al_ready = sem("a_ready"), sem("ah_ready"), sem("al_ready")
    fgate_dve, fgate_act, fc_out = sem("fgate_dve"), sem("fgate_act"), sem("fc_out")
    cb_in = [sem("cb_in0"), sem("cb_in1")]
    q_raw, q_sq, q_sum, q_ms, q_rs, fg_ready = (
        sem(n) for n in ("q_raw", "q_sq", "q_sum", "q_ms", "q_rs", "fg_ready"))
    f_src, f_trs, f_v, f_g, f_th, f_epi = (sem(n) for n in ("f_src", "f_trs", "f_v", "f_g", "f_th", "f_epi"))
    fs_full, fs_read, fmx, fp_exp, fp_ready, ft_full, ft_out, fpv, fo_free, fy = (
        sem(n) for n in ("fs_full", "fs_read", "fmx", "fp_exp", "fp_ready", "ft_full", "ft_out", "fpv", "fo_free",
                         "fy"))
    oh_ready, ol_ready = sem("oh_ready"), sem("ol_ready")
    out_done = sem("out_done")

    def col(name, n=0, rows=slice(0, P)):
        return PAR[rows, bass.ds(COL[name] + n, 1)]

    def blk(t, n):
        return t[:, bass.ds(n, 1), :].rearrange("p o s -> p (o s)")

    block = nc.Block()
    block.__enter__()

    @block.sync
    def _(sp):
        def load(u0, j, i, per, src, width):
            s = (u0 + j) % NSLOT
            if u0 + j >= NSLOT:
                sp.wait_ge(lo_ready, i * per + (u0 + j - NSLOT + 1))
            sp.dma_start(RAW[:, s, 0:width], src).then_inc(raw_full[s], 16)

        def stream(name, w, iters, per):
            with sp.Fori(0, iters) as i:
                for j in range(per):
                    load(U[name], j, i, per, w[bass.ds(i * per + j, 1), :, :].rearrange("o p n -> p (o n)"), UW)

        def stream_down(name, w):
            with sp.Fori(0, 2) as i:
                for j in range(12):
                    k0 = sum(DOWN_KC[:j % 3]) * P
                    kw = DOWN_KC[j % 3] * P
                    load(U[name], j, i, 12,
                         w[bass.ds(i * 4 + j // 3, 1), :, k0:k0 + kw].rearrange("o p n -> p (o n)"), kw)

        sp.dma_start(PAR[:], A["par"]).then_inc(par_in, 16)
        sp.dma_start(MEMT[:], A["mem"]).then_inc(mem_in, 16)
        for u in range(NATT):
            load(0, u, 0, 0, A["w_att"][u, :, :], UW)
            if u < 4:
                sp.dma_start(X[:, 2 * u:2 * u + 2, :], A["x"][:, 2 * u:2 * u + 2, :]).then_inc(x_in[u], 16)
            if UNITS[u] in BIAS_AFTER:
                p = BIAS_AFTER[UNITS[u]]
                if p == 0:
                    sp.wait_ge(unit_done, 8)
                if p >= 2:
                    sp.wait_ge(s_read, 2 * (SIDX[("na", p - 2, 3)] + 1))
                sp.dma_start(BN[:, p % 2, :, :, :], A["rpb"][p, :, :, :, :]).then_inc(bias_in[p % 2], 16)
            heads = {("mlq", 1): (0,), ("mlq", 2): (1, 2, 3)}.get(UNITS[u], ())
            if heads:
                sp.wait_ge(gates_out, 32)
                if heads[0] == 0:
                    sp.wait_ge(v_ready, VEV[("gate", 0)] + 1)
                else:
                    sp.wait_ge(o_free, 2 + 4)
                for h in heads:
                    for g in range(2):
                        for d in range(2):
                            row = gates_d[g, 32 * d + h, :]
                            sp.dma_start(UE[:, UE_AT[h], 2 * g + d, :], row.partition_broadcast(P)).then_inc(ue_in, 16)
        for j in range(6):
            c0 = 3 * UW + j % 3 * (UW // 2)
            load(U["merge"], j, 0, 0, A["w_mrg"][j // 3, :, c0:c0 + UW // 2], UW // 2)
        with sp.Fori(1, 4) as i:
            for j in range(12):
                n, r = j // 6, j % 6
                wd = UW if r < 3 else UW // 2
                c0 = r * UW if r < 3 else 3 * UW + (r - 3) * wd
                load(UM, j, i, 12,
                     A["w_mrg"][bass.ds(i * 2 + n, 1), :, c0:c0 + wd].rearrange("o p n -> p (o n)"), wd)
        stream("out", A["w_out"], 2, 4)
        stream("up0", A["w_up0"], 11, 4)
        stream_down("down0", A["w_down0"])
        stream("ain", A["w_ain"], 6, 4)
        stream("aout", A["w_aout"], 2, 4)
        stream("up1", A["w_up1"], 11, 4)
        stream_down("down1", A["w_down1"])
        load(U["f"], 0, 0, 0, A["w_f"], UW)
        for p in range(FA_PAIRS + 1):
            for j in range(4):
                if p < FA_PAIRS:
                    load(U["fa"], 4 * p + j, 0, 0, A["w_fa"][4 * p + j, :, :], UW)
                if p >= 1 and j == 1:
                    pp = p - 1
                    if pp == 0:
                        sp.wait_ge(fc_out, 16)
                    if pp >= 2:
                        sp.wait_ge(fs_read, 8 * (pp - 1))
                    for h in range(2):
                        sp.dma_start(CB[:, pp % 2, h, :], fc_d[2 * pp + h, :].partition_broadcast(P))\
                            .then_inc(cb_in[pp % 2], 16)
        stream("bout", A["w_bout"], 2, 4)
        stream("up2", A["w_up2"], 11, 4)
        stream_down("down2", A["w_down2"])
        for n in range(KB):
            sp.wait_ge(lin_free, O["down2"] + n + 3)
            sp.dma_start(out[n, :, :], X[:, n, :]).then_inc(out_done, 16)
        sp.wait_ge(out_done, 16 * KB)

    @block.gpsimd
    def _(pool):
        def lo(u0, j, i, per):
            s = (u0 + j) % NSLOT
            pool.wait_ge(hi_ready, i * per + (u0 + j + 1))
            nc.gpsimd.tensor_tensor(WL[:, s, :], RAW[:, s, :], WH[:, s, :].bitcast(F32), ALU.subtract)\
                .then_inc(lo_ready, 1)

        def los(name, iters, per):
            with pool.Fori(0, iters) as i:
                for j in range(per):
                    lo(U[name], j, i, per)

        for t, v in ((ONES, 1.0), (BLK, 0.0), (IDN, 0.0), (LO, 1.0), (UP, 1.0), (NM, 0.0), (EPSC, EPS), (ZERO, 0.0)):
            nc.gpsimd.memset(t[:], v).then_inc(consts, 1)
        pool.wait_ge(consts, 8)
        nc.gpsimd.memset(EPSC[:, 1:2], EPS * EPS)
        nc.gpsimd.memset(BLK[0:64, 0:64], 1.0)
        pool.drain()
        nc.gpsimd.memset(BLK[64:128, 64:128], 1.0)
        pool.drain()
        nc.gpsimd.affine_select(out=IDN[:], in_=IDN[:], compare_op=ALU.not_equal, fill=1.0, base=0,
                                pattern=[[-1, P]], channel_multiplier=1)
        nc.gpsimd.affine_select(out=LO[:], in_=LO[:], compare_op=ALU.is_ge, fill=0.0, base=0,
                                pattern=[[1, P]], channel_multiplier=-1)
        nc.gpsimd.affine_select(out=UP[:], in_=UP[:], compare_op=ALU.is_ge, fill=0.0, base=0,
                                pattern=[[-1, P]], channel_multiplier=1)
        for half in range(2):
            r = slice(64 * half, 64 * half + 64)
            pool.drain()
            nc.gpsimd.affine_select(out=NM[r], in_=NM[r], compare_op=ALU.is_ge, fill=NEG, base=0,
                                    pattern=[[-64, 2], [1, P]], channel_multiplier=-1)
        pool.drain().then_inc(masks, 1)
        for u in range(NATT):
            lo(0, u, 0, 0)
            if UNITS[u] in BIAS_AFTER:
                p = BIAS_AFTER[UNITS[u]]
                pool.wait_ge(bias_in[p % 2], 16 * (p // 2 + 1))
                for half in range(2):
                    r = BN[64 * half:64 * half + 64, p % 2, :, :, :].rearrange("p a m j -> p (a m) j")
                    low = r[:, :, 0:48]
                    nc.gpsimd.affine_select(out=low, in_=low, compare_op=ALU.is_ge, fill=NEG, base=8,
                                            pattern=[[0, 28], [1, 48]], channel_multiplier=-1)
                    pool.drain()
                for half in range(2):
                    r = BN[64 * half:64 * half + 64, p % 2, :, :, :].rearrange("p a m j -> p (a m) j")
                    high = r[:, :, 16:64]
                    nc.gpsimd.affine_select(out=high, in_=high, compare_op=ALU.is_ge, fill=NEG, base=7 - 16,
                                            pattern=[[0, 28], [-1, 48]], channel_multiplier=1)\
                        .then_inc(bias_ready, 1)
                    pool.drain()
        for j in range(6):
            lo(U["merge"], j, 0, 0)
        with pool.Fori(1, 4) as i:
            for j in range(12):
                lo(UM, j, i, 12)
        los("out", 2, 4)
        los("up0", 11, 4)
        los("down0", 2, 12)
        los("ain", 6, 4)
        los("aout", 2, 4)
        los("up1", 11, 4)
        los("down1", 2, 12)
        lo(U["f"], 0, 0, 0)
        los("fa", 8, 4)
        los("bout", 2, 4)
        los("up2", 11, 4)
        los("down2", 2, 12)

    @block.scalar
    def _(act):
        A_ = nc.scalar.activation

        def hi(u0, j, i, per):
            if not isinstance(i, int) or u0 + j + i * per < NUNITS:
                s = (u0 + j) % NSLOT
                act.wait_ge(raw_full[s], i * (16 * per // NSLOT) + 16 * ((u0 + j) // NSLOT + 1))
                if u0 + j >= NSLOT:
                    act.wait_ge(unit_done, i * per + (u0 + j - NSLOT + 1))
                A_(WH[:, s, :], RAW[:, s, :], ACT.Copy).then_inc(hi_ready, 1)

        AHEAD = 3
        LN_EXP = "natural_log_exp_and_others"

        def split(src, n, name, g, dst, width=S):
            c = SPL[name] + n
            if c >= 2:
                act.wait_ge(split_ready, c - 1)
            A_((SQ, TE)[c % 2][:, 0:width], src, ACT.Square)
            A_(dst, src, ACT.Identity, scale=g).then_inc(sq_ready, 1)

        def rstd(name, dst, width, inv):
            if name != "down0":
                act.preload_act_table_set(LN_EXP)
            act.wait_ge(norm_sum, NORM[name] + 1)
            A_(TE[:, 0:width], NB[:, 0:width], ACT.Ln, scale=inv, bias=EPSC[:, 0:1])
            act.drain()
            A_(dst, TE[:, 0:width], ACT.Exp, scale=-0.5).then_inc(r_ready, 1)

        act.preload_act_table_set(LN_EXP)
        act.wait_ge(par_in, 16)
        act.wait_ge(mem_in, 16)
        for n in range(KB):
            split(MEMT[:, n, :], n, "mem", col("mem_g", n), MH[:, n, :], M)

        def x_split(n):
            if n % 2 == 0:
                act.wait_ge(x_in[n // 2], 16)
            split(X[:, n, :], n, "x", col("mix_g", n), XH[:, n, :])

        for n in range(AHEAD):
            hi(0, n, 0, 0)
        act.wait_ge(masks, 1)
        rstd("mem", RM[:], M, 1.0 / D)
        act.drain()
        x_split(0)
        x_split(1)

        for t, (un, st) in enumerate(SLOTS):
            u = UIDX[un] if un else None
            if un:
                hi(0, u + AHEAD, 0, 0)
            if t < 6:
                x_split(t + 2)
            if un == ("xq", 0):
                act.drain()
                rstd("x", R[:], S, 1.0 / D)
                act.wait_ge(par_ready, 1)
                A_(GE[:], GE[:], ACT.Ln, bias=EPSC[:, 0:1])
                act.drain()
                A_(GE[:], GE[:], ACT.Exp, scale=0.5)
            if st and st[0] in ("xa", "na"):
                g = SIDX[st]
                nk = M if st[0] == "xa" else S
                for j in range(2):
                    act.wait_ge(mx_ready, 2 * g + j + 1)
                    A_(SX[:, j, 0:nk], SX[:, j, 0:nk], ACT.Exp, bias=NX[:, j:j + 1],
                       accum_out=RS[:, j:j + 1]).then_inc(p_exp, 1)
            if st and st[0] == "ml":
                m = 4 * st[1] + st[2]
                s = st[2]
                act.wait_ge(e_arg, m + 1)
                A_(SX[:, 0, P * s:S], SX[:, 0, P * s:S], ACT.Exp, scale=-1.0)
                A_(SX[:, 1, 0:P * (s + 1)], SX[:, 1, 0:P * (s + 1)], ACT.Exp, scale=-1.0).then_inc(e_ready, 1)
            if st and st[0] in ("ml", "end") and st[1] >= 1:
                h = st[1] - 1
                if st[2] == 2:
                    act.wait_ge(h_ready, h + 1)
                    A_(SQ[:], FI[:, 0, :], ACT.Square).then_inc(h_sq, 1)
                if st[2] == 3:
                    act.wait_ge(h_sum, h + 1)
                    act.preload_act_table_set(LN_EXP)
                    A_(TD[:], TD[:], ACT.Ln, scale=1.0 / P, bias=EPSC[:, 0:1])
                    act.drain()
                    A_(TD[:], TD[:], ACT.Exp, scale=-0.5).then_inc(h_rs, 1)
            if un and un[0] in HALF:
                k = sum(1 for x in UNITS[:u] if x[0] in HALF)
                act.wait_ge(half_act, k + 1)
                if un[0] == "mlo":
                    A_(SO[:, un[1] % 2, :], TA[:], ACT.Tanh, scale=0.5).then_inc(y_arg, 1)
                elif un[0] == "mg":
                    q = un[1]
                    A_(EG[:, q, :], TA[:], ACT.Tanh, scale=0.5, bias=HB[:, q % 3 * 8 + q // 3:q % 3 * 8 + q // 3 + 1])\
                        .then_inc(y_arg, 1)
                else:
                    A_(TA[:], TC[:], ACT.Tanh, scale=0.5).then_inc(y_arg, 1)
            if t == GATE_T + 1:
                act.wait_ge(gate_dve, 1)
                A_(GT[:, 2, :], GT[:, 2, :], ACT.Abs)
                act.drain()
                A_(GT[:, 2, :], GT[:, 2, :], ACT.Exp, scale=-1.0)
                act.drain()
                A_(GT[:, 2, :], GT[:, 2, :], ACT.Ln, bias=ONES[0:64, 0:1]).then_inc(gate_act, 1)
            if t == GATE_T + 4:
                act.wait_ge(gate_dve, 2)
                A_(GU[:, 1, :], GU[:, 1, :], ACT.Exp, scale=-1.0).then_inc(gate_act, 1)
                act.wait_ge(gate_act, 2)
                act.dma_start(gates_d[0, :, :], GU[:, 0, :]).then_inc(gates_out, 16)
                act.dma_start(gates_d[1, :, :], GU[:, 1, :]).then_inc(gates_out, 16)
            if st and st[0] in ("xa", "na"):
                g = SIDX[st]
                nk = M if st[0] == "xa" else S
                for j in range(2):
                    act.wait_ge(t_full, 2 * g + j + 1)
                    if g >= 1:
                        act.wait_ge(pv_done, 2 * g + j - 1)
                    A_(PT[:, j, 0:nk], TRB[j][:, 0:nk], ACT.Copy).then_inc(t_out, 1)
        for n in range(12):
            act.wait_ge(y_ready, n + 1)
            if n == 0:
                act.wait_ge(y_done, ML_H)
            A_(YH[:, n, :], Y[:, n, :], ACT.Copy).then_inc(yh_ready, 1)
        def merged_hi(i, n):
            act.wait_ge(mrg, i * 2 + (n + 1))
            A_(blk(GH, i * 2 + n), TA[:], ACT.Copy).then_inc(mrg_hi, 1)

        for n in range(2):
            for b in range(3):
                hi(U["merge"], 3 * n + b + AHEAD, 0, 0)
            merged_hi(0, n)
        with act.Fori(1, 4) as i:
            for n in range(2):
                for b in range(3):
                    hi(UM, 6 * n + b + AHEAD, i, 12)
                    act.wait_ge(mg_arg, i * 6 + (3 * n + b - 5))
                    A_(TC[:] if b == 0 else TD[:] if b == 1 else TE[:], TA[:], ACT.Tanh, scale=0.5,
                       bias=HB[:, bass.ds(i * 2 + (b * 8 + n), 1)]).then_inc(mg_act, 1)
                for b in range(3):
                    hi(UM, 6 * n + 3 + b + AHEAD, i, 12)
                merged_hi(i, n)

        def residual(name, iters, per, outs, gain, last=False, between=None):
            def body(i, at_end):
                for j in range(per):
                    if not (at_end and j + AHEAD >= per):
                        hi(U[name], j + AHEAD, i, per)
                    if (j + 1) % (per // outs) == 0:
                        n = j // (per // outs)
                        nn = i * outs + n
                        if not last:
                            act.wait_ge(lin_free, i * outs + (O[name] + n + 3))
                            act.wait_ge(split_ready, i * outs + (SPL[name] + n))
                            A_(blk(XH, nn), blk(X, nn), ACT.Identity, scale=col(gain, nn))
                            if name == "down0":
                                A_(TE[:], blk(X, nn), ACT.Square, scale=GE[:, bass.ds(nn, 1)])
                            A_(SQ[:], blk(X, nn), ACT.Square).then_inc(sq_ready, 1)
            if last:
                body(0, False)
                body(1, True)
            else:
                with act.Fori(0, iters) as i:
                    body(i, False)
                act.wait_ge(split_ready, SPL[name] + KB)
                if name == "down0":
                    act.preload_act_table_set(LN_EXP)
                    act.wait_ge(fin_sum, 1)
                    A_(TD[:], bank[6][:], ACT.Ln, scale=1.0 / D, bias=EPSC[:, 1:2])
                    act.wait_ge(norm_sum, NORM[name] + 1)
                    act.drain()
                    A_(SS[:], TD[:], ACT.Exp, scale=-0.5)
                if between:
                    between()
                rstd(name, R[:], S, 1.0 / D)

        def up(name, l, iters, fn):
            with act.Fori(0, iters) as i:
                for n in range(2):
                    hi(U[name], 2 * n + AHEAD, i, 4)
                    act.wait_ge(conv_ready, i * 2 + (FB * l + n + 1))
                    A_(TD[:], TC[:], fn).then_inc(glu_ready, 1)
                    hi(U[name], 2 * n + 1 + AHEAD, i, 4)
                    act.wait_ge(ff_ready, i * 2 + (FB * l + n + 1))
                    A_(blk(FH, i * 2 + n), TA[:], ACT.Copy).then_inc(ffh_ready, 1)

        residual("out", 2, 4, 4, "fg0")
        up("up0", 0, 11, ACT.Gelu_apprx_tanh)
        residual("down0", 2, 12, 4, "ag0")
        with act.Fori(0, 2) as i:
            for n in range(4):
                for r in range(3):
                    hi(U["ain"], 3 * n + r + AHEAD, i, 12)
                act.wait_ge(a_ready, i * 4 + (n + 1))
                A_(blk(AH, i * 4 + n), TA[:], ACT.Copy).then_inc(ah_ready, 1)
        residual("aout", 2, 4, 4, "fg1")
        up("up1", 1, 11, ACT.Silu)
        def other_split():
            act.wait_ge(unit_done, U["f"])
            with act.Fori(0, KB) as i:
                A_(blk(AH, i), blk(X, i), ACT.Identity, scale=col("ag1", i)).then_inc(ah_ready, 1)

        residual("down1", 2, 12, 4, "kvg", between=other_split)
        hi(U["f"], AHEAD, 0, 0)
        A_(NMR[:], NM[:], ACT.Copy)
        A_(IDR[:], IDN[:], ACT.Copy)
        act.drain()

        def o_split(n):
            act.wait_ge(fy, n + 1)
            if n == 0:
                act.wait_ge(unit_done, U["bout"])
            A_(AH[:, n, :], FY[:, n, :], ACT.Copy).then_inc(oh_ready, 1)

        for p in range(FA_PAIRS + 1):
            for s in range(4):
                if p < FA_PAIRS:
                    hi(U["fa"], 4 * p + s + AHEAD, 0, 0)
                if p >= 1:
                    g = 4 * (p - 1) + s
                    nk = P * (s + 1)
                    for j in range(2):
                        act.wait_ge(fmx, 2 * g + j + 1)
                        A_(FX[:, j, 0:nk], FX[:, j, 0:nk], ACT.Exp, bias=NX[:, j:j + 1],
                           accum_out=RS[:, j:j + 1]).then_inc(fp_exp, 1)
                if p < FA_PAIRS and s in (1, 2):
                    act.wait_ge(q_ms, 2 * p + s)
                    A_(TD[:], SS[:], ACT.Ln)
                    act.drain()
                    A_(TD[:], TD[:], ACT.Exp, scale=-0.5).then_inc(q_rs, 1)
                if p < FA_PAIRS and s < 2:
                    act.wait_ge(q_raw, 2 * p + s + 1)
                    A_(SQ[:], TA[:], ACT.Square).then_inc(q_sq, 1)
                if p == 0 and s == 0:
                    act.wait_ge(fgate_dve, 1)
                    A_(FC[:, 2, :], FC[:, 2, :], ACT.Abs)
                    act.drain()
                    A_(FC[:, 2, :], FC[:, 2, :], ACT.Exp, scale=-1.0)
                    act.drain()
                    A_(FC[:, 2, :], FC[:, 2, :], ACT.Ln, bias=ONES[0:16, 0:1]).then_inc(fgate_act, 1)
                if p == 0 and s == 2:
                    act.wait_ge(fgate_dve, 2)
                    act.dma_start(fc_d[:, :], FC[:, 1, :]).then_inc(fc_out, 16)
                if p < FA_PAIRS and s == 3:
                    act.wait_ge(f_g, p + 1)
                    A_(TE[:], TC[:], ACT.Exp, scale=-1.0).then_inc(f_th, 1)
                    act.drain()
                    A_(TE[:], TE[:], ACT.Ln, bias=ONES[:, 0:1])
                    act.drain()
                    A_(FG[:, p % 2, :], TE[:], ACT.Exp, scale=-1.0).then_inc(fg_ready, 1)
                if p >= 1:
                    for j in range(2):
                        act.wait_ge(ft_full, 2 * g + j + 1)
                        if g >= 1:
                            act.wait_ge(fpv, 2 * g + j - 1)
                        A_(FP[:, j, 0:nk], TRB[j][:, 0:nk], ACT.Copy).then_inc(ft_out, 1)
                if p == FA_PAIRS and s >= 1:
                    o_split(2 * s - 2)
                    o_split(2 * s - 1)
        for n in (6, 7):
            o_split(n)
        residual("bout", 2, 4, 4, "fg2")
        up("up2", 2, 11, ACT.Silu)
        residual("down2", 2, 12, 4, None, last=True)

    @block.vector
    def _(dve):
        v = nc.vector

        def split(src, n, name, g, h, l, width=S, acc=SS):
            c = SPL[name] + n
            dve.wait_ge(sq_ready, c + 1)
            v.tensor_tensor(acc[:, 0:width], acc[:, 0:width], (SQ, TE)[c % 2][:, 0:width], ALU.add)
            v.scalar_tensor_tensor(out=l, in0=src, scalar=g, in1=h.bitcast(F32), op0=ALU.mult,
                                   op1=ALU.subtract).then_inc(split_ready, 1)

        dve.sem_inc(lin_free, 2)
        v.memset(SS[:], 0.0)
        v.memset(TD[:, 0:M], 0.0)
        dve.wait_ge(par_in, 16)
        v.tensor_scalar(HB[:], PAR[:, COL["bmg"]:COL["bmg"] + 24], 0.5, None, ALU.mult)
        mlg = PAR[:, COL["mlg"]:COL["mlg"] + ML_H]
        v.tensor_scalar(mlg, mlg, 0.5, None, ALU.mult)
        ag = PAR[:, COL["ag0"]:COL["ag0"] + KB]
        fin = PAR[:, COL["fin"]:COL["fin"] + KB]
        v.tensor_tensor(ag, ag, fin, ALU.mult)
        v.tensor_tensor(GE[:], fin, fin, ALU.mult)
        v.tensor_scalar(PAR[:, COL["qn"]:COL["qn"] + 1], PAR[:, COL["qn"]:COL["qn"] + 1], 0.125, None, ALU.mult)
        dve.drain().then_inc(par_ready, 1)
        for n in range(KB):
            split(MEMT[:, n, :], n, "mem", col("mem_g", n), MH[:, n, :], ML[:, n, :], M, TD)
            dve.drain()

        def x_split(n):
            split(X[:, n, :], n, "x", col("mix_g", n), XH[:, n, :], XL[:, n, :])
            dve.drain()

        def read_lin(ev, out_, in1, scalar=None):
            b = LB[LEV[ev] % 2]
            if scalar is None:
                v.tensor_tensor(out_, b[:, 0:in1.shape[1]], in1, ALU.mult).then_inc(lin_free, 1)
            else:
                v.scalar_tensor_tensor(out=out_, in0=b[:, 0:in1.shape[1]], scalar=scalar, in1=in1, op0=ALU.mult,
                                       op1=ALU.mult).then_inc(lin_free, 1)

        def conv3(c, taps, n, bias, off):
            mid = 0 - off
            w = [col(x, n) for x in taps]
            if bias is not None:
                v.tensor_scalar(TC[:], c[:], w[mid], col(bias, n), ALU.mult, ALU.add)
            else:
                v.tensor_scalar(TC[:], c[:], w[mid], None, ALU.mult)
            last = None
            for k in range(3):
                d = k + off
                if d == 0:
                    continue
                dve.drain()
                if d < 0:
                    last = v.scalar_tensor_tensor(out=TC[:, -d:S], in0=c[:, 0:S + d], scalar=w[k],
                                                  in1=TC[:, -d:S], op0=ALU.mult, op1=ALU.add)
                else:
                    last = v.scalar_tensor_tensor(out=TC[:, 0:S - d], in0=c[:, d:S], scalar=w[k],
                                                  in1=TC[:, 0:S - d], op0=ALU.mult, op1=ALU.add)
            return last

        halfs = 0
        extras = 0
        MC = 0.25 * 128 ** -0.5
        for t, (un, st) in enumerate(SLOTS):
            if un in (("memk", 0), ("xq", 0)):
                dve.wait_ge(r_ready, 1 if un[0] == "memk" else 2)
            if st and st[0] == "ml":
                h, s = st[1], st[2]
                m = 4 * h + s
                if m % 4 == 0:
                    dve.wait_ge(ue_in, 64 * (h + 1))
                if m == 0:
                    dve.wait_ge(t_full, 2 * len(STEPS))
                v.tensor_scalar(SX[:, 0, P * s:S], UE[:, UE_AT[h], 0, P * s:S], UT[:, s, h:h + 1], 0.0,
                                ALU.subtract, ALU.max)
                v.tensor_scalar(SX[:, 1, 0:P * (s + 1)], UE[:, UE_AT[h], 1, 0:P * (s + 1)], UT[:, s, 32 + h:33 + h], 0.0,
                                ALU.subtract, ALU.max).then_inc(e_arg, 1)
            if st and st[0] in ("xa", "na"):
                g = SIDX[st]
                nk = M if st[0] == "xa" else S
                if st[0] == "na" and st[2] == 0:
                    dve.wait_ge(bias_ready, 2 * (st[1] + 1))
                for j in range(2):
                    dve.wait_ge(s_full, 2 * g + j + 1)
                    if g >= 1:
                        dve.wait_ge(t_full, 2 * g + j - 1)
                    if st[0] == "xa":
                        b = ZERO[:]
                    else:
                        b = BN[:, st[1] % 2, j, 6 - 2 * st[2]:14 - 2 * st[2], :].rearrange("p m c -> p (m c)")
                    v.tensor_tensor_reduce(out=SX[:, j, 0:nk], in0=SB[j][:, 0:nk], in1=b, scale=1.0, scalar=NEG,
                                           op0=ALU.add, op1=ALU.max, accum_out=MX[:, j:j + 1]).then_inc(s_read, 1)
                    dve.drain()
                    v.tensor_scalar(NX[:, j:j + 1], MX[:, j:j + 1], -1.0, None, ALU.mult).then_inc(mx_ready, 1)
            if st and st[2] == 0 and t > 0 and SLOTS[t - 1][1] is not None and SLOTS[t - 1][1][0] in ("xa", "na"):
                pk, pp, _ = SLOTS[t - 1][1]
                dve.wait_ge(pv_done, 2 * SIDX[(pk, pp, 3)] + 2)
                if pk == "xa":
                    v.tensor_copy(Y[:, 8 + 2 * pp, :], OB[0][:]).then_inc(y_ready, 1)
                    v.tensor_copy(Y[:, 9 + 2 * pp, :], OB[1][:]).then_inc(o_free, 1)
                else:
                    v.tensor_copy(Y[:, pp, :], OB[0][:]).then_inc(o_free, 1)
            if st and st[0] in ("xa", "na"):
                for j in range(2):
                    dve.wait_ge(p_exp, 2 * g + j + 1)
                    v.reciprocal(RI[:, j:j + 1], RS[:, j:j + 1])
                    dve.drain()
                    v.tensor_scalar(SX[:, j, 0:nk], SX[:, j, 0:nk], RI[:, j:j + 1], None, ALU.mult)\
                        .then_inc(p_ready, 1)
            if st and st[0] == "ml":
                dve.wait_ge(e_ready, m + 1)
                dve.wait_ge(ms_full, m + 1)
                if m >= 2:
                    dve.wait_ge(mpv_done, m - 1)
                if m == 0:
                    dve.wait_ge(pv_done, 2 * len(STEPS))
                    v.memset(PB[:, 2, P:S], 0.0)
                b = SB[m % 2]
                pb = 2 if s == 0 else s % 2
                v.scalar_tensor_tensor(out=PT[:, m % 2, P * s:S], in0=b[:, P * s:S], scalar=MC,
                                       in1=SX[:, 0, P * s:S], op0=ALU.mult, op1=ALU.mult)
                v.scalar_tensor_tensor(out=PB[:, pb, 0:P * (s + 1)], in0=b[:, 0:P * (s + 1)], scalar=MC,
                                       in1=SX[:, 1, 0:P * (s + 1)], op0=ALU.mult, op1=ALU.mult).then_inc(ms_read, 1)
                dve.drain()
                dg = slice(P * s, P * (s + 1))
                v.tensor_tensor(PT[:, m % 2, dg], PT[:, m % 2, dg], LO[:], ALU.mult)
                v.tensor_tensor(PB[:, pb, dg], PB[:, pb, dg], UP[:], ALU.mult).then_inc(mp_ready, 1)
            if st and st[0] in ("ml", "end") and st[1] >= 1:
                h, s = st[1] - 1, st[2]
                if s == 0:
                    dve.wait_ge(mpv_done, 4 * h + 4)
                    v.scalar_tensor_tensor(out=FI[:, 0, :], in0=bank[5][:], scalar=-1.0, in1=UE[:, UE_AT[h], 2, :],
                                           op0=ALU.mult, op1=ALU.max)
                    v.scalar_tensor_tensor(out=FI[:, 1, :], in0=bank[7][:], scalar=-1.0, in1=UE[:, UE_AT[h], 3, :],
                                           op0=ALU.mult, op1=ALU.max)
                    dve.drain()
                    v.tensor_tensor(FI[:, 0, :], bank[5][:], FI[:, 0, :], ALU.max)
                    v.tensor_tensor(FI[:, 1, :], bank[7][:], FI[:, 1, :], ALU.max)
                    v.tensor_copy(TE[:], bank[4][:])
                    v.tensor_copy(SS[:], bank[6][:]).then_inc(nd_free, 1)
                if s == 1:
                    dve.drain()
                    v.reciprocal(FI[:, 0, :], FI[:, 0, :])
                if s == 2:
                    v.reciprocal(FI[:, 1, :], FI[:, 1, :])
                    dve.drain()
                    v.tensor_tensor(FI[:, 0, :], FI[:, 0, :], TE[:], ALU.mult)
                    v.tensor_tensor(FI[:, 1, :], FI[:, 1, :], SS[:], ALU.mult)
                    dve.drain()
                    v.tensor_tensor(FI[:, 0, :], FI[:, 0, :], FI[:, 1, :], ALU.add).then_inc(h_ready, 1)
            for e in PRE[t]:
                extras += 1
                dve.wait_ge(extra_full, extras)
                v.tensor_copy(TD[:], LB[LEV[e] % 2][:]).then_inc(lin_free, 1)
                dve.drain().then_inc(h_sum, 1)
                v.scalar_tensor_tensor(out=FI[:, 0, :], in0=SO[:, e[1] % 2, :], scalar=1.0, in1=FI[:, 0, :],
                                       op0=ALU.add, op1=ALU.mult)
                dve.drain()
            if un:
                kind, n = un
                dve.wait_ge(unit_done, UIDX[un] + 1)
                trs = [e[0] for e in EXTRA[t]]
                if "tr" in trs:
                    dve.wait_ge(extra_full, extras + trs.index("tr") + 1)
                if kind == "memk":
                    read_lin(un, MK[:, n, :], RM[:])
                elif kind == "xq":
                    read_lin(un, XQ[:, n, :], R[:], 128 ** -0.5)
                elif kind == "naq":
                    read_lin(un, QN[:, n % 2, :], R[:], 0.125)
                elif kind == "nak":
                    read_lin(un, KN[:, n % 2, :], R[:])
                elif kind in ("memv", "nav", "mlv"):
                    w = M if kind == "memv" else S
                    read_lin(un, TC[:, 0:w], RM[:] if kind == "memv" else R[:])
                    dve.drain().then_inc(v_src, 1)
                elif kind == "gate":
                    read_lin(un, TA[:], R[:])
                    dve.drain()
                    v.tensor_scalar(GT[:, 0, :], TA[0:64, :], col("gb", 0, slice(0, 64)), None, ALU.add)
                    v.tensor_scalar(TA[64:128, :], TA[64:128, :], col("gb", 0, slice(64, 128)), None, ALU.add)
                    dve.drain()
                    v.tensor_scalar(GT[:, 1, :], TA[64:128, :], 0.0, None, ALU.min)
                    v.tensor_copy(GT[:, 2, :], TA[64:128, :]).then_inc(gate_dve, 1)
                elif kind in ("mlq", "mlk"):
                    read_lin(un, TA[:], R[:])
                    dve.drain()
                    c = n if kind == "mlq" else 4 + n
                    conv3(TA, ("mlc0", "mlc1", "mlc2"), c, "mlb", -1).then_inc(half_act, 1)
                    halfs += 1
                    dve.wait_ge(y_arg, halfs)
                    v.scalar_tensor_tensor(out=(Q if kind == "mlq" else K)[:, n % 2, :], in0=TA[:], scalar=1.0,
                                           in1=TC[:], op0=ALU.add, op1=ALU.mult)
                elif kind in ("mlo", "mg"):
                    read_lin(un, TA[:], R[:])
                    dve.drain().then_inc(half_act, 1)
                    halfs += 1
                    dve.wait_ge(y_arg, halfs)
                dve.drain().then_inc(epi_done, 1)
            if t < 6:
                for n in ((0, 1, 2) if t == 0 else (t + 2,)):
                    x_split(n)
            if t == GATE_T + 2:
                dve.wait_ge(gate_act, 1)
                v.tensor_tensor(GT[:, 1, :], GT[:, 1, :], GT[:, 2, :], ALU.subtract)
                v.memset(TE[0:64, :], 1.0)
                dve.drain()
                v.tensor_tensor_scan(GT[0:32, 2, :], TE[0:32, :], GT[0:32, 1, :], 0.0, ALU.mult, ALU.add)
                v.tensor_tensor_scan(GT[32:64, 2, ::-1], TE[32:64, :], GT[32:64, 1, ::-1], 0.0, ALU.mult,
                                     ALU.add)
            if t == GATE_T + 3:
                v.tensor_tensor(GT[:, 3, :], GT[:, 0, :], GT[:, 2, :], ALU.subtract)
                dve.drain()
                v.tensor_tensor_scan(GU[0:32, 0, :], GT[0:32, 3, :], GT[0:32, 3, :], NEG, ALU.max, ALU.max)
                v.tensor_tensor_scan(GU[32:64, 0, ::-1], GT[32:64, 3, ::-1], GT[32:64, 3, ::-1], NEG, ALU.max,
                                     ALU.max)
                dve.drain()
                v.tensor_tensor(GU[:, 1, :], GT[:, 2, :], GU[:, 0, :], ALU.add).then_inc(gate_dve, 1)
                dve.drain().then_inc(v_src, 1)
            for e in EXTRA[t]:
                extras += 1
                dve.wait_ge(extra_full, extras)
                b = LB[LEV[e] % 2]
                kind, n = e[1:]
                if kind == "memv":
                    d, w = MV[:, :, n * P:(n + 1) * P], M
                elif kind == "nav":
                    d, w = VN[:, n % 2, :, :], S
                elif kind == "mlv":
                    d, w = V[:, n % 2, :, :], S
                else:
                    d, w = UT[:], 4 * 64
                v.tensor_copy(d, b[:, 0:w].rearrange("p (t c) -> p t c", c=d.shape[2])).then_inc(lin_free, 1)
                dve.drain().then_inc(v_ready, 1)
            if PRE[t]:
                h = PRE[t][0][1]
                dve.wait_ge(h_rs, h + 1)
                v.scalar_tensor_tensor(out=Y[:, 4 + h, :], in0=FI[:, 0, :], scalar=col("mlg", h), in1=TD[:],
                                       op0=ALU.mult, op1=ALU.mult).then_inc(y_done, 1)
                dve.drain()
        dve.sem_inc(y_ready, 12 - 2)
        for n in range(12):
            dve.wait_ge(yh_ready, n + 1)
            v.tensor_tensor(YL[:, n, :], Y[:, n, :], YH[:, n, :].bitcast(F32), ALU.subtract).then_inc(mrg_lo, 1)
        def merge_block(i, n, gates, u0, o0, j0):
            for b in range(3):
                g = gates[b]
                dve.wait_ge(unit_done, i * 12 + (u0 + j0 + b + 1))
                v.scalar_tensor_tensor(out=g, in0=g, scalar=1.0, in1=LB[(o0 + j0 + b) % 2][:],
                                       op0=ALU.add, op1=ALU.mult).then_inc(lin_free, 1)
                dve.drain()
                if b == 1:
                    v.tensor_tensor(gates[0], gates[0], gates[1], ALU.add)
            v.tensor_tensor(gates[0], gates[0], gates[2], ALU.add)
            dve.drain()
            v.tensor_scalar(TA[:], gates[0], 0.5, None, ALU.mult).then_inc(mrg, 1)
            dve.wait_ge(mrg_hi, i * 2 + (n + 1))
            v.tensor_tensor(blk(GL, i * 2 + n), TA[:], blk(GH, i * 2 + n).bitcast(F32), ALU.subtract)\
                .then_inc(mrg_lo, 1)
            dve.drain()

        for n in range(2):
            merge_block(0, n, [EG[:, 3 * n + b, :] for b in range(3)], U["merge"], O["merge"], 3 * n)
        with dve.Fori(1, 4) as i:
            for n in range(2):
                for b in range(3):
                    j = 6 * n + b
                    dve.wait_ge(unit_done, i * 12 + (UM + j + 1))
                    v.tensor_tensor(TA[:], LB[(OM + j) % 2][:], R[:], ALU.mult).then_inc(lin_free, 1)
                    dve.drain().then_inc(mg_arg, 1)
                    dve.wait_ge(mg_act, i * 6 + (3 * n + b - 5))
                merge_block(i, n, (TC[:], TD[:], TE[:]), UM, OM, 6 * n + 3)

        def residual(name, iters, per, outs, gain, last=False, between=None):
            v.memset(SS[:], 0.0)
            if name == "down0":
                v.memset(TC[:], 0.0)
            dve.drain()
            with dve.Fori(0, iters) as i:
                for n in range(outs):
                    nn = i * outs + n
                    dve.wait_ge(unit_done, i * per + (U[name] + (n + 1) * per // outs))
                    v.tensor_tensor(blk(X, nn), blk(X, nn), LB[(O[name] + n) % 2][:], ALU.add).then_inc(lin_free, 1)
                    if not last:
                        dve.drain()
                        dve.wait_ge(sq_ready, i * outs + (SPL[name] + n + 1))
                        v.tensor_tensor(SS[:], SS[:], SQ[:], ALU.add)
                        if name == "down0":
                            v.tensor_tensor(TC[:], TC[:], TE[:], ALU.add)
                        v.scalar_tensor_tensor(out=blk(XL, nn), in0=blk(X, nn), scalar=col(gain, nn),
                                               in1=blk(XH, nn).bitcast(F32), op0=ALU.mult, op1=ALU.subtract)\
                            .then_inc(split_ready, 1)
            if between:
                between()
            if not last:
                dve.wait_ge(r_ready, NORM[name] + 1)

        def up(name, l, iters, off, taps, bias):
            with dve.Fori(0, iters) as i:
                for n in range(2):
                    nn = i * 2 + n
                    dve.wait_ge(unit_done, i * 4 + (U[name] + 2 * n + 1))
                    v.tensor_tensor(TA[:], LB[0 if (O[name] % 2) == 0 else 1][:], R[:], ALU.mult)\
                        .then_inc(lin_free, 1)
                    dve.drain()
                    conv3(TA, taps, nn, bias, off).then_inc(conv_ready, 1)
                    dve.wait_ge(unit_done, i * 4 + (U[name] + 2 * n + 2))
                    v.tensor_tensor(TE[:], LB[1 if (O[name] % 2) == 0 else 0][:], R[:], ALU.mult)\
                        .then_inc(lin_free, 1)
                    dve.drain()
                    dve.wait_ge(glu_ready, i * 2 + (FB * l + n + 1))
                    v.tensor_tensor(TA[:], TE[:], TD[:], ALU.mult).then_inc(ff_ready, 1)
                    dve.wait_ge(ffh_ready, i * 2 + (FB * l + n + 1))
                    v.tensor_tensor(blk(FL, nn), TA[:], blk(FH, nn).bitcast(F32), ALU.subtract).then_inc(ffl_ready, 1)
                    dve.drain()

        residual("out", 2, 4, 4, "fg0")
        up("up0", 0, 11, -1, ("fc00", "fc01", "fc02"), "fb0")
        residual("down0", 2, 12, 4, "ag0")
        with dve.Fori(0, 2) as i:
            for n in range(4):
                for r, dst in enumerate((TE, TD, TA)):
                    j = 3 * n + r
                    dve.wait_ge(unit_done, i * 12 + (U["ain"] + j + 1))
                    v.tensor_tensor(dst[:], LB[(O["ain"] + j) % 2][:], SS[:], ALU.mult).then_inc(lin_free, 1)
                v.scalar_tensor_tensor(out=blk(X, i * 4 + n), in0=blk(X, i * 4 + n), scalar=col("fin", i * 4 + n),
                                       in1=R[:], op0=ALU.mult, op1=ALU.mult)
                dve.drain()
                v.tensor_tensor(TA[:], TA[:], TD[:], ALU.mult)
                dve.drain()
                conv3(TA, ("ac0", "ac1", "ac2"), i * 4 + n, None, -2)
                dve.drain()
                v.tensor_tensor(TA[:], TC[:], TE[:], ALU.mult).then_inc(a_ready, 1)
                dve.wait_ge(ah_ready, i * 4 + (n + 1))
                v.tensor_tensor(blk(AL, i * 4 + n), TA[:], blk(AH, i * 4 + n).bitcast(F32), ALU.subtract)\
                    .then_inc(al_ready, 1)
                dve.drain()
        residual("aout", 2, 4, 4, "fg1")
        up("up1", 1, 11, -2, ("fc10", "fc11", "fc12"), None)
        def other_split():
            with dve.Fori(0, KB) as i:
                dve.wait_ge(ah_ready, i + (KB + 1))
                v.scalar_tensor_tensor(out=blk(AL, i), in0=blk(X, i), scalar=col("ag1", i),
                                       in1=blk(AH, i).bitcast(F32), op0=ALU.mult, op1=ALU.subtract)\
                    .then_inc(al_ready, 1)

        residual("down1", 2, 12, 4, "kvg", between=other_split)
        dve.wait_ge(unit_done, U["f"] + 1)
        v.tensor_tensor(TA[0:16, :], LB[O["f"] % 2][0:16, :], R[0:16, :], ALU.mult).then_inc(lin_free, 1)
        dve.drain()
        v.tensor_scalar(TA[0:16, :], TA[0:16, :], col("bf", 0, slice(0, 16)), None, ALU.add)
        dve.drain()
        v.tensor_scalar(FC[:, 0, :], TA[0:16, :], 0.0, None, ALU.min)
        v.tensor_copy(FC[:, 2, :], TA[0:16, :]).then_inc(fgate_dve, 1)
        v.memset(TE[0:16, :], 1.0)
        dve.drain()

        def o_split(n):
            dve.wait_ge(oh_ready, n + 1)
            v.tensor_tensor(AL[:, n, :], FY[:, n, :], AH[:, n, :].bitcast(F32), ALU.subtract).then_inc(ol_ready, 1)

        def o_gate(pp):
            dve.wait_ge(fpv, 8 * (pp + 1))
            dve.wait_ge(fg_ready, pp + 1)
            v.tensor_tensor(FY[:, pp, :], OB[0][:], FG[:, pp % 2, :], ALU.mult).then_inc(fo_free, 1)
            dve.drain().then_inc(fy, 1)

        for p in range(FA_PAIRS + 1):
            o0 = O["fa"] + FA_L * p
            for s in range(4):
                if p >= 1:
                    pp = p - 1
                    g = 4 * pp + s
                    nk = P * (s + 1)
                    if s == 0:
                        dve.wait_ge(cb_in[pp % 2], 32 * (pp // 2 + 1))
                    for j in range(2):
                        dve.wait_ge(fs_full, 2 * g + j + 1)
                        if g >= 1:
                            dve.wait_ge(ft_full, 2 * g + j - 1)
                        v.tensor_tensor_reduce(out=FX[:, j, 0:nk], in0=SB[j][:, 0:nk], in1=CB[:, pp % 2, j, 0:nk],
                                               scale=1.0, scalar=NEG, op0=ALU.add, op1=ALU.max,
                                               accum_out=MX[:, j:j + 1]).then_inc(fs_read, 1)
                        dve.drain()
                        v.tensor_scalar(NX[:, j:j + 1], MX[:, j:j + 1], -1.0, None, ALU.mult).then_inc(fmx, 1)
                    for j in range(2):
                        dve.wait_ge(fp_exp, 2 * g + j + 1)
                        v.reciprocal(RI[:, j:j + 1], RS[:, j:j + 1])
                        dve.drain()
                        v.tensor_scalar(FX[:, j, 0:nk], FX[:, j, 0:nk], RI[:, j:j + 1], None, ALU.mult)\
                            .then_inc(fp_ready, 1)
                if p < FA_PAIRS:
                    if s in (1, 2):
                        dve.wait_ge(q_sum, 2 * p + s)
                        v.tensor_scalar(SS[:], LB[(o0 + (1, 3)[s - 1]) % 2][:], 1.0 / 64, EPSC[:, 0:1], ALU.mult,
                                        ALU.add).then_inc(lin_free, 1)
                        dve.drain().then_inc(q_ms, 1)
                        dve.wait_ge(q_rs, 2 * p + s)
                        v.tensor_tensor(SS[:], SS[:], TD[:], ALU.mult)
                        v.scalar_tensor_tensor(out=TA[:], in0=TA[:], scalar=col("kn" if s == 1 else "qn"),
                                               in1=TD[:], op0=ALU.mult, op1=ALU.mult)
                        dve.drain()
                        v.tensor_tensor(SS[:], SS[:], TD[:], ALU.mult)
                        dve.drain()
                        v.tensor_scalar(SS[:], SS[:], -0.5, 1.5, ALU.mult, ALU.add)
                        dve.drain()
                        v.tensor_tensor((FK if s == 1 else FQ)[:, p % 2, :], TA[:], SS[:], ALU.mult)\
                            .then_inc(f_epi, 1)
                        dve.drain()
                    if s == 3:
                        dve.wait_ge(f_trs, p + 1)
                        v.tensor_copy(FV[:, p % 2, :, :], LB[(o0 + 5) % 2][:].rearrange("p (t c) -> p t c", c=P))\
                            .then_inc(lin_free, 1)
                        dve.drain().then_inc(f_v, 1)
                    dve.wait_ge(unit_done, U["fa"] + 4 * p + s + 1)
                    b = LB[(o0 + (0, 2, 4, 6)[s]) % 2]
                    if s < 2:
                        v.tensor_tensor(TA[:], b[:], R[:], ALU.mult).then_inc(lin_free, 1)
                        dve.drain().then_inc(q_raw, 1)
                        if p == 0 and s == 1:
                            dve.wait_ge(fgate_act, 1)
                            v.tensor_tensor(FC[:, 0, :], FC[:, 2, :], FC[:, 0, :], ALU.subtract)
                            dve.drain()
                            v.tensor_tensor_scan(FC[:, 1, :], TE[0:16, :], FC[:, 0, :], 0.0, ALU.mult, ALU.add)\
                                .then_inc(fgate_dve, 1)
                    elif s == 2:
                        if p:
                            dve.wait_ge(f_th, p)
                        v.tensor_tensor(TC[:], b[:], R[:], ALU.mult).then_inc(lin_free, 1)
                        dve.drain().then_inc(f_src, 1)
                    else:
                        v.tensor_tensor(TC[:], b[:], R[:], ALU.mult).then_inc(lin_free, 1)
                        dve.drain()
                        v.tensor_scalar(TC[:], TC[:], -87.0, None, ALU.max)
                        dve.drain().then_inc(f_g, 1)
                if p >= 2 and s == 0:
                    o_gate(p - 2)
                if p == FA_PAIRS and s >= 1:
                    o_split(2 * s - 2)
                    o_split(2 * s - 1)
        o_split(6)
        o_gate(7)
        o_split(7)
        residual("bout", 2, 4, 4, "fg2")
        up("up2", 2, 11, -2, ("fc20", "fc21", "fc22"), None)
        residual("down2", 2, 12, 4, None, last=True)

    @block.tensor
    def _(pe):
        mm = nc.tensor.matmul

        def unit(u0, j, i, per, kc, xh, xl, k0, dst, start=True, stop=True, width=S, ready=None, before_last=None):
            s = (u0 + j) % NSLOT
            pe.wait_ge(lo_ready, i * per + (u0 + j + 1))
            for k in range(kc):
                if before_last and k == kc - 1:
                    before_last()
                if ready:
                    pe.wait_ge(ready[0], ready[1] + k + 1)
                w = slice(k * P, (k + 1) * P)
                a, b = xh[:, k0 + k, 0:width], xl[:, k0 + k, 0:width]
                mm(dst[:, 0:width], WH[:, s, w], a, start=start and k == 0, stop=False)
                mm(dst[:, 0:width], WH[:, s, w], b, start=False, stop=False)
                last = mm(dst[:, 0:width], WL[:, s, w], a, start=False, stop=stop and k == kc - 1)
            last.then_inc(unit_done, 1)

        def norm(name, src, width, total):
            pe.wait_ge(split_ready, total)
            if NORM[name]:
                pe.wait_ge(r_ready, NORM[name])
            if name == "down0":
                mm(bank[6][:], ONES[:], TC[:], start=True, stop=True).then_inc(fin_sum, 1)
            mm(NB[:, 0:width], ONES[:], src, start=True, stop=True).then_inc(norm_sum, 1)

        pe.wait_ge(consts, 8)
        pe.wait_ge(masks, 1)

        def need(un):
            pe.wait_ge(epi_done, UIDX[un] + 1)

        extras = 0

        def products(st):
            kind, p, s = st
            g = SIDX[st]
            for j in range(2):
                pe.wait_ge(t_out, 2 * g + j + 1)
                if s == 0 and j == 0:
                    pe.wait_ge(v_ready, VEV[("memv", 3)] + 1 if kind == "xa" else VEV[("nav", p)] + 1)
                    done = p if kind == "xa" else 2 + p
                    if done:
                        pe.wait_ge(o_free, done)
                nb = MB if kind == "xa" else TB
                for k in range(nb):
                    if kind == "xa":
                        dst = OB[j][:, P * s:P * (s + 1)]
                        w = MV[:, k, (2 * p + j) * P:(2 * p + j + 1) * P]
                    else:
                        dst = OB[0][64 * j:64 * j + 64, P * s:P * (s + 1)]
                        w = VN[:, p % 2, k, 64 * j:64 * j + 64]
                    last = mm(dst, w, PT[:, j, k * P:(k + 1) * P], start=k == 0, stop=k == nb - 1)
                last.then_inc(pv_done, 1)

        def ml_products(h, s):
            m = 4 * h + s
            pe.wait_ge(mp_ready, m + 1)
            if s == 0:
                pe.wait_ge(v_ready, VEV[("mlv", h)] + 1)
                if h == 0:
                    pe.wait_ge(o_free, 6)
                    pe.wait_ge(t_out, 2 * len(STEPS))
                else:
                    pe.wait_ge(nd_free, h)
            fw = PT[:, m % 2, P * s:S]
            mm(bank[4][:, P * s:S], V[:, h % 2, s, :], fw, start=s == 0, stop=s == 3)
            mm(bank[5][:, P * s:S], ONES[:], fw, start=s == 0, stop=s == 3)
            w = S if s == 0 else P * (s + 1)
            bw = PB[:, 2 if s == 0 else s % 2, 0:w]
            mm(bank[6][:, 0:w], V[:, h % 2, s, :], bw, start=s == 0, stop=s == 3)
            mm(bank[7][:, 0:w], ONES[:], bw, start=s == 0, stop=s == 3).then_inc(mpv_done, 1)

        for t, (un, st) in enumerate(SLOTS):
            before = SLOTS[t - 1][1] if t else None
            if st and st[0] in ("xa", "na"):
                kind, p, s = st
                g = SIDX[st]
                if s == 0:
                    need(("xq", 3) if kind == "xa" else ("nak", p))
                for j in range(2):
                    if g >= 1:
                        pe.wait_ge(s_read, 2 * g + j - 1)
                    if kind == "xa":
                        h = 2 * p + j
                        mm(SB[j][:, 0:M], XQ[:, h, P * s:P * (s + 1)], MK[:, h, :], start=True, stop=True)\
                            .then_inc(s_full, 1)
                    else:
                        r = slice(64 * j, 64 * j + 64)
                        mm(SB[j][:], QN[r, p % 2, P * s:P * (s + 1)], KN[r, p % 2, :], start=True, stop=True)\
                            .then_inc(s_full, 1)
            if st and st[0] == "ml":
                _, h, s = st
                m = 4 * h + s
                if s == 0:
                    need(("mlk", h))
                if m == 0:
                    pe.wait_ge(s_read, 2 * len(STEPS))
                if m >= 2:
                    pe.wait_ge(ms_read, m - 1)
                mm(SB[m % 2][:], K[:, h % 2, P * s:P * (s + 1)], Q[:, h % 2, :], start=True, stop=True)\
                    .then_inc(ms_full, 1)
            if before and before[0] in ("xa", "na"):
                products(before)
            if before and before[0] == "ml":
                ml_products(before[1], before[2])
            for e in PRE[t]:
                pe.wait_ge(lin_free, LEV[e] + 1)
                pe.wait_ge(h_sq, e[1] + 1)
                mm(LB[LEV[e] % 2][:], ONES[:], SQ[:], start=True, stop=True).then_inc(extra_full, 1)
            if un:
                o = LEV[un]
                pe.wait_ge(lin_free, o + 1)
                if un[0] in ("memk", "memv"):
                    unit(0, UIDX[un], 0, 0, KB, MH, ML, 0, LB[o % 2], width=M,
                         ready=(split_ready, SPL["mem"]) if t == 0 else None)
                else:
                    unit(0, UIDX[un], 0, 0, KB, XH, XL, 0, LB[o % 2],
                         ready=(split_ready, SPL["x"]) if un == ("xq", 0) else None)
                if t == 0:
                    norm("mem", TD[:, 0:M], M, SPL["mem"] + KB)
                if un == ("xq", 0):
                    norm("x", SS[:], S, SPL["x"] + KB)
            for e in EXTRA[t]:
                o = LEV[e]
                pe.wait_ge(lin_free, o + 1)
                if e[1] == "gate":
                    pe.wait_ge(v_src, VEV[e[1:]] + 1)
                    for k in range(TB):
                        last = nc.tensor.transpose(LB[o % 2][:, 64 * k:64 * k + 64], GT[:, 3, P * k:P * (k + 1)],
                                                   IDN[0:64, 0:64])
                else:
                    pe.wait_ge(v_src, VEV[e[1:]] + 1)
                    src = TC
                    for k in range(MB if e[1] == "memv" else TB):
                        last = nc.tensor.transpose(LB[o % 2][:, P * k:P * (k + 1)], src[:, P * k:P * (k + 1)], IDN[:])
                last.then_inc(extra_full, 1)
            if st and st[0] in ("xa", "na"):
                for j in range(2):
                    pe.wait_ge(p_ready, 2 * g + j + 1)
                    if g >= 1:
                        pe.wait_ge(t_out, 2 * g + j - 1)
                    for k in range(MB if kind == "xa" else TB):
                        last = nc.tensor.transpose(TRB[j][:, P * k:P * (k + 1)], SX[:, j, P * k:P * (k + 1)], IDN[:])
                    last.then_inc(t_full, 1)
        def branch(u0, o0, j, i, b):
            pe.wait_ge(lin_free, i * 12 + (o0 + j + 1))
            unit(u0, j, i, 12, 4, YH, YL, (4, 0, 8)[b], LB[(o0 + j) % 2])

        pe.wait_ge(mrg_lo, 12)
        for j in range(6):
            branch(U["merge"], O["merge"], j, 0, j % 3)
        with pe.Fori(1, 4) as i:
            for j in range(12):
                if j % 6 < 3:
                    pe.wait_ge(lin_free, i * 12 + (OM + j + 1))
                    unit(UM, j, i, 12, KB, XH, XL, 0, LB[(OM + j) % 2])
                else:
                    branch(UM, OM, j, i, j % 6 - 3)

        def linear(name, iters, per, xh, xl, ready, norm_of=None, before_last=None):
            def body(i, first):
                for j in range(per):
                    pe.wait_ge(lin_free, i * per + (O[name] + j + 1))
                    if first and j == 0:
                        unit(U[name], j, i, per, KB, xh, xl, 0, LB[O[name] % 2], ready=ready,
                             before_last=before_last)
                        if norm_of:
                            norm(norm_of, SS[:], S, SPL[norm_of] + KB)
                    else:
                        unit(U[name], j, i, per, KB, xh, xl, 0, LB[(O[name] + j) % 2])

            body(0, True)
            with pe.Fori(1, iters) as i:
                body(i, False)

        def down(name, l):
            with pe.Fori(0, 2) as i:
                for j in range(12):
                    if j % 3 == 0:
                        pe.wait_ge(lin_free, i * 4 + (O[name] + j // 3 + 1))
                    k0 = sum(DOWN_KC[:j % 3])
                    unit(U[name], j, i, 12, DOWN_KC[j % 3], FH, FL, k0, LB[(O[name] + j // 3) % 2],
                         start=j % 3 == 0, stop=j % 3 == 2, ready=(ffl_ready, FB * l + k0) if j < 3 else None)

        def after(name):
            return (split_ready, SPL[name])

        linear("out", 2, 4, GH, GL, (mrg_lo, 12))
        linear("up0", 11, 4, XH, XL, after("out"), "out")
        down("down0", 0)
        linear("ain", 2, 12, XH, XL, after("down0"), "down0")
        linear("aout", 2, 4, AH, AL, (al_ready, 0))
        linear("up1", 11, 4, XH, XL, after("aout"), "aout")
        down("down1", 1)
        pe.wait_ge(lin_free, O["f"] + 1)
        unit(U["f"], 0, 0, 0, KB, XH, XL, 0, LB[O["f"] % 2], ready=after("down1"))
        norm("down1", SS[:], S, SPL["down1"] + KB)

        def f_products(pp, s):
            g = 4 * pp + s
            for j in range(2):
                pe.wait_ge(ft_out, 2 * g + j + 1)
                if s == 0 and j == 0:
                    pe.wait_ge(f_v, pp + 1)
                    if pp:
                        pe.wait_ge(fo_free, pp)
                for k in range(s + 1):
                    last = mm(OB[0][64 * j:64 * j + 64, P * s:P * (s + 1)], FV[:, pp % 2, k, 64 * j:64 * j + 64],
                              FP[:, j, k * P:(k + 1) * P], start=k == 0, stop=k == s)
                last.then_inc(fpv, 1)

        for p in range(FA_PAIRS + 1):
            o0 = O["fa"] + FA_L * p
            for s in range(4):
                if p >= 1:
                    pp = p - 1
                    g = 4 * pp + s
                    nk = P * (s + 1)
                    if s == 0:
                        pe.wait_ge(f_epi, 2 * p)
                    for j in range(2):
                        if g >= 1:
                            pe.wait_ge(fs_read, 2 * g + j - 1)
                        r = slice(64 * j, 64 * j + 64)
                        mm(SB[j][:, 0:nk], FQ[r, pp % 2, P * s:P * (s + 1)], FK[r, pp % 2, 0:nk], start=True,
                           stop=False)
                        for h in range(2):
                            last = mm(SB[j][:, P * s + 64 * h:P * s + 64 * h + 64], NMR[r, h, :], IDR[r, r],
                                      start=False, stop=h == 1)
                        last.then_inc(fs_full, 1)
                if p < FA_PAIRS:
                    o = o0 + (0, 1, 3, 5)[s]
                    pe.wait_ge(lin_free, o + 1)
                    if s in (1, 2):
                        pe.wait_ge(q_sq, 2 * p + s)
                        mm(LB[o % 2][:], BLK[:], SQ[:], start=True, stop=True).then_inc(q_sum, 1)
                    if s == 3:
                        pe.wait_ge(f_src, p + 1)
                        for k in range(TB):
                            last = nc.tensor.transpose(LB[o % 2][:, P * k:P * (k + 1)], TC[:, P * k:P * (k + 1)],
                                                       IDN[:])
                        last.then_inc(f_trs, 1)
                    if s >= 1:
                        o += 1
                        pe.wait_ge(lin_free, o + 1)
                    xh, xl = ((XH, XL), (AH, AL), (XH, XL), (AH, AL))[s]
                    unit(U["fa"], 4 * p + s, 0, 0, KB, xh, xl, 0, LB[o % 2],
                         ready=(al_ready, KB) if p == 0 and s == 1 else None)
                if p >= 1:
                    if s >= 1:
                        f_products(pp, s - 1)
                    elif p >= 2:
                        f_products(pp - 1, 3)
                    for j in range(2):
                        pe.wait_ge(fp_ready, 2 * g + j + 1)
                        if g >= 1:
                            pe.wait_ge(ft_out, 2 * g + j - 1)
                        for k in range(s + 1):
                            last = nc.tensor.transpose(TRB[j][:, P * k:P * (k + 1)], FX[:, j, P * k:P * (k + 1)],
                                                       IDN[:])
                        last.then_inc(ft_full, 1)
        linear("bout", 2, 4, AH, AL, (ol_ready, 0), before_last=lambda: f_products(FA_PAIRS - 1, 3))
        linear("up2", 11, 4, XH, XL, after("bout"), "bout")
        down("down2", 2)

    block.__exit__(None, None, None)


def _units(w):
    k, n = w.shape
    return np.ascontiguousarray(w.reshape(k // P, P, n // P, P).transpose(2, 1, 0, 3).reshape(n // P, P, k))


def _cols(v):
    return np.asarray(v).reshape(-1, P).T


def kernel(**inp):
    import concourse.bacc as bacc
    from concourse.bass_utils import run_bass_kernel_spmd
    g = {k: np.asarray(v) for k, v in inp.items()}
    w_in = g["w_in"][0]
    c_ml, c_g, c_na, c_xa, c_mg = 0, 2048, 2064, 3600, 4112
    ml = [_units(w_in[:, c_ml + 512 * k:c_ml + 512 * (k + 1)]) for k in range(4)]
    na = [_units(w_in[:, c_na + 512 * k:c_na + 512 * (k + 1)]) for k in range(3)]
    xq = _units(w_in[:, c_xa:c_xa + 512])
    kv = _units(g["w_mem_kv"][0])
    wg = np.zeros((D, P), np.float32)
    gb = np.zeros((P,), np.float32)
    bi, bf = g["b_ml_igate"][0], g["b_ml_fgate"][0]
    for q, (src, b) in enumerate(((0, bi[0]), (2, bi[1]), (1, bf[0]), (3, bf[1]))):
        wg[:, 32 * q:32 * q + 4] = w_in[:, c_g + 4 * src:c_g + 4 * src + 4]
        gb[32 * q:32 * q + 4] = b
    of = {"memk": kv[0:4], "memv": kv[4:8], "xq": xq, "naq": na[0], "nak": na[1], "nav": na[2],
          "gate": _units(wg), "mlq": ml[0], "mlk": ml[1], "mlv": ml[2], "mlo": ml[3]}
    mg = _units(w_in[:, c_mg:])
    of["mg"] = [mg[q % 3 * 8 + q // 3] for q in range(6)]
    w_att = np.stack([of[k][n] for k, n in UNITS])
    br = [_units(g[k][0]) for k in ("w_br_ml", "w_br_na", "w_br_xa")]
    w_mrg = np.stack([np.concatenate([mg[n], mg[8 + n], mg[16 + n], br[0][n], br[1][n], br[2][n]], axis=1)
                      for n in range(KB)])

    def pairs(w, parts):
        u = _units(w)
        n = len(u) // parts
        return np.ascontiguousarray(u.reshape(parts, n, P, -1).transpose(1, 0, 2, 3).reshape(parts * n, P, -1))

    wkvf, wqg = g["w_kvf_2"], g["b_w_qg_2"][0]
    uk, uv = _units(wkvf[:, 0:D]), _units(wkvf[:, D:2 * D])
    uq, ug = _units(wqg[:, 0:D]), _units(wqg[:, D:])
    w_fa = np.stack([x[p] for p in range(FA_PAIRS) for x in (uk, uq, uv, ug)])
    wf = np.zeros((D, P), np.float32)
    wf[:, 0:16] = wkvf[:, 2 * D:]
    bfc = np.zeros((P,), np.float32)
    bfc[0:16] = g["b_f_2"]
    pad = np.zeros((8, RPB_R, RPB_W), np.float32)
    pad[:, :, GRID - 16:GRID - 16 + RPB_C] = g["na_rpb"][0]
    rpb = np.zeros((8, 2, GRID, 14, GRID), np.float32)
    for half in range(2):
        for c in range(GRID):
            rpb[:, half, c] = pad[:, 1 - half:15 - half, GRID - 1 - c:2 * GRID - 1 - c]
    rpb = rpb.reshape(NA_PAIRS, 2, P, 14, GRID).transpose(0, 2, 1, 3, 4)
    par = {"mix_g": g["mix_norm_g"][0], "mem_g": g["mem_norm_g"][0], "mlb": g["b_ml_conv"][0],
           "mlg": g["ml_norm_g"][0], "bmg": g["b_merge_gate"][0], "fg0": g["ffn_norm_g"][0],
           "fb0": g["b_ffn_conv"][0], "gb": gb, "ag0": g["attn_norm_2"][0], "ag1": g["attn_norm_2"][1],
           "fg1": g["ffn_norm_2"][0], "fg2": g["ffn_norm_2"][1], "kvg": g["kv_norm_2"], "bf": bfc,
           "kn": np.tile(g["k_norm_2"], 2), "qn": np.tile(g["q_norm_2"][0], 2)}
    par["fin"] = g["final_norm_g"]
    for k in range(3):
        par[f"mlc{k}"] = g["w_ml_conv"][0, k]
        par[f"fc0{k}"] = g["w_ffn_conv"][0, k]
        par[f"ac{k}"] = g["a_conv_2"][0, k]
        par[f"fc1{k}"] = g["ffn_conv_2"][0, k]
        par[f"fc2{k}"] = g["ffn_conv_2"][1, k]
    feat = lambda a: np.ascontiguousarray(a.T.reshape(KB, P, -1).transpose(1, 0, 2))
    arrays = {
        "x": feat(g["x"][0]), "mem": feat(g["mem"][0]),
        "par": np.ascontiguousarray(np.concatenate([_cols(par[n]) for n, _ in _COLS], axis=1)),
        "rpb": np.ascontiguousarray(rpb), "w_att": w_att, "w_mrg": w_mrg, "w_out": _units(g["w_out"][0]),
        "w_up0": pairs(g["w_ffn_up"][0], 2), "w_down0": _units(g["w_ffn_down"][0]),
        "w_ain": pairs(g["a_w_in_2"][0], 3), "w_aout": _units(g["a_w_out_2"][0]),
        "w_up1": pairs(g["ffn_w_up_2"][0], 2), "w_down1": _units(g["ffn_w_down_2"][0]),
        "w_f": _units(wf)[0], "w_fa": w_fa, "w_bout": _units(g["b_w_out_2"][0]),
        "w_up2": pairs(g["ffn_w_up_2"][1], 2), "w_down2": _units(g["ffn_w_down_2"][1]),
    }
    nc = bacc.Bacc("TRN2", target_bir_lowering=False, num_devices=1)
    aps = {k: nc.dram_tensor("in_" + k, a.shape, F32, kind="ExternalInput").ap() for k, a in arrays.items()}
    out = nc.dram_tensor("out_x", (KB, P, S), F32, kind="ExternalOutput").ap()
    two_blocks(nc, aps, out)
    r = run_bass_kernel_spmd(nc, [{"in_" + k: a for k, a in arrays.items()}], core_ids=[0])
    return np.ascontiguousarray(r.results[0]["out_x"].reshape(D, S).T)[None]
```

```python
import numpy as np
import concourse.bass as bass
from concourse import mybir

F32 = mybir.dt.float32
F32R = mybir.dt.float32r
ALU = mybir.AluOpType
ACT = mybir.ActivationFunctionType
AX = mybir.AxisListType

P = 128
D = 1024
KB = D // P
S = 512
TB = S // P
M = 256
MB = M // P
F = 2816
FB = F // P
NSLOT = 4
UW = KB * P
EPS = 1e-6
NEG = -1e30
ML_H, XA_H, FA_PAIRS, NA_PAIRS = 4, 4, 8, 4
ROWS, GRID = 8, 64
QC, KC = P // ROWS, M // ROWS
KEY0 = (0, 64, 192, 256)
VAR = (0, 1, 1, 2)
VCH = 7
DOWN_KC = (8, 7, 7)

_COLS = [("mix_g", KB), ("mem_g", KB), ("mlc0", 8), ("mlc1", 8), ("mlc2", 8), ("mlb", 8), ("mlg", 4),
         ("bmg", 24), ("fg0", KB), ("fc00", FB), ("fc01", FB), ("fc02", FB), ("fb0", FB), ("gb", 1),
         ("ag0", KB), ("ag1", KB), ("fg1", KB), ("fg2", KB), ("ac0", KB), ("ac1", KB), ("ac2", KB), ("kvg", KB),
         ("bf", 1), ("kn", 1), ("qn", 1), ("fc10", FB), ("fc11", FB), ("fc12", FB), ("fc20", FB), ("fc21", FB),
         ("fc22", FB), ("fin", KB)]
COL, NCOL = {}, 0
for _n, _w in _COLS:
    COL[_n] = NCOL
    NCOL += _w

SLOTS = []
for _n in range(4):
    SLOTS.append((("memk", _n), None))
for _n in range(4):
    SLOTS.append((("memv", _n), None))
for _n in range(2):
    SLOTS.append((("xq", _n), None))
for _j, _un in enumerate((("xq", 2), ("xq", 3), ("naq", 0), ("nak", 0), ("nav", 0), ("gate", 0), None, None)):
    SLOTS.append((_un, ("xa", _j // 4, _j % 4)))
for _p in range(3):
    for _s, _un in enumerate((("naq", _p + 1), ("nak", _p + 1), ("nav", _p + 1), None)):
        SLOTS.append((_un, ("na", _p, _s)))
for _s, _un in enumerate(("mlq", "mlk", "mlv", "mlo")):
    SLOTS.append(((_un, 0), ("na", 3, _s)))
for _h in range(3):
    for _s, _un in enumerate(("mlq", "mlk", "mlv", "mlo")):
        SLOTS.append(((_un, _h + 1), ("ml", _h, _s)))
for _q in range(8):
    SLOTS.append((("mg", _q) if _q < 6 else ("br", _q - 6), ("ml", 3, _q) if _q < 4 else ("end", 4, _q - 4)))


def finishing(st):
    if not st or st[0] not in ("ml", "end") or st[1] == 0:
        return ()
    return (st[2],) if st[0] == "ml" else ((0, 1), (2,), (), (3,))[st[2]]


UNITS = [u for u, _ in SLOTS if u is not None]
UIDX = {u: n for n, u in enumerate(UNITS)}
NATT = len(UNITS)
BIAS_AFTER = {("naq", 0): 0, ("naq", 1): 1, ("naq", 3): 2, ("mlq", 0): 3}
STEPS = [s for _, s in SLOTS if s is not None and s[0] in ("xa", "na")]
SIDX = {s: n for n, s in enumerate(STEPS)}
LEV = {}
VEV = {}
VSRC = {}
EXTRA = []
GATE_T = [_un for _un, _ in SLOTS].index(("gate", 0))
_prev = None
for _t, (_un, _st) in enumerate(SLOTS):
    _ex = [("hn", _st[1] - 1)] if 3 in finishing(_st) else []
    if _prev is not None and _prev[0] in ("memv", "nav", "mlv"):
        _ex.append(("tr",) + _prev)
        if _prev[0] == "nav":
            _ex.append(("tr", "nav64", _prev[1]))
    if _t == GATE_T + 4:
        _ex.append(("tr", "gate", 0))
    for _e in ([_un] if _un else []) + _ex:
        LEV[_e] = len(LEV)
        if _e[0] == "tr":
            VEV[_e[1:]] = len(VEV)
            if _e[1] != "nav64":
                VSRC[_e[1:]] = len(VSRC)
    EXTRA.append(_ex)
    _prev = _un
NL1 = len(LEV)

U, O = {}, {}
_u, _o = NATT, NL1
for _n, _nu, _no in (("merge", 40, 40), ("out", 8, 8), ("up0", 44, 44), ("down0", 24, 8), ("ain", 24, 24),
                     ("aout", 8, 8), ("up1", 44, 44), ("down1", 24, 8), ("f", 1, 1), ("fa", 32, 0)):
    U[_n], O[_n] = _u, _o
    _u, _o = _u + _nu, _o + _no
UM, OM = U["merge"] - 8, O["merge"] - 8
FA_L = 7
_o = O["fa"] + FA_L * FA_PAIRS
for _n, _nu, _no in (("bout", 8, 8), ("up2", 44, 44), ("down2", 24, 8)):
    U[_n], O[_n] = _u, _o
    _u, _o = _u + _nu, _o + _no
NUNITS = _u
HALF = ("mlq", "mlk", "mlo", "mg")
SPL = {"mem": 0, "x": 8, "out": 16, "down0": 24, "aout": 32, "down1": 40, "bout": 48}
NORM = {"mem": 0, "x": 1, "out": 2, "down0": 3, "aout": 4, "down1": 5, "bout": 6}


def two_blocks(nc, A, out):
    base = (nc.sbuf_base + 63) // 64 * 64
    top = [base]

    def fixed(name, shape, dt=F32):
        t = nc.alloc_sbuf_tensor_at(name, shape, dt, offset=top[0])
        n = 4
        for d in shape[1:]:
            n *= d
        top[0] += (n + 31) // 32 * 32
        return t

    X = fixed("X", [P, KB, S])
    XH = fixed("XH", [P, KB, S], F32R)
    XL = fixed("XL", [P, KB, S], F32R)
    RAW = fixed("RAW", [P, NSLOT, UW])
    WH = fixed("WH", [P, NSLOT, UW], F32R)
    WL = fixed("WL", [P, NSLOT, UW], F32R)
    R = fixed("R", [P, S])
    RM = fixed("RM", [P, M])
    SS = fixed("SS", [P, S])
    SQ = fixed("SQ", [P, S])
    TA = fixed("TA", [P, S])
    TC = fixed("TC", [P, S])
    TD = fixed("TD", [P, S])
    TE = fixed("TE", [P, S])
    ONES = fixed("ONES", [P, P])
    BLK = fixed("BLK", [P, P])
    IDN = fixed("IDN", [P, P])
    LO = fixed("LO", [P, P])
    UP = fixed("UP", [P, P])
    PAR = fixed("PAR", [P, NCOL])
    HB = fixed("HB", [P, 24])
    UT = fixed("UT", [P, TB, 64])
    EPSC = fixed("EPSC", [P, 2])
    GE = fixed("GE", [P, KB])
    MX = fixed("MX", [P, 2])
    NX = fixed("NX", [P, 2])
    RS = fixed("RS", [P, 2])
    RI = fixed("RI", [P, 2])
    zone = top[0]
    assert zone + 91 * 1024 <= nc.sbuf_usable_end, (zone, nc.sbuf_usable_end)

    def at(name, kib, shape, dt=F32):
        n = 4
        for d in shape[1:]:
            n *= d
        assert kib * 1024 + n <= 91 * 1024
        return nc.alloc_sbuf_tensor_at(name, shape, dt, offset=zone + int(kib * 1024))

    NM = at("NM", 90, [P, 2, P])
    Y = at("Y", 0, [P, 12, S])
    MEMT = at("MEMT", 0, [P, KB, M])
    SX = at("SX", 24, [P, 2, S])
    PT = at("PT", 28, [P, 2, S])
    PB = at("PB", 32, [P, 3, S])
    ZERO = at("ZERO", 32, [P, M])
    GU = at("GU", 34, [64, 2, S])
    Q = at("Q", 38, [P, 2, S])
    SO = at("SO", 42, [P, 2, S])
    V = at("V", 46, [P, 2, TB, P])
    K = at("K", 50, [P, 2, S])
    XQ = at("XQ", 38, [P, 4, S])
    MK = at("MK", 46, [P, 4, M])
    MV = at("MV", 50, [P, MB, 4 * P])
    GT = at("GT", 54, [64, 4, S])
    UE = at("UE", 54, [P, ML_H, 4, S])
    MH = at("MH", 62, [P, KB, M], F32R)
    ML = at("ML", 70, [P, KB, M], F32R)
    QN = at("QN", 62, [P, 2, S])
    KN = at("KN", 66, [P, 2, S])
    VN = at("VN", 70, [P, 2, VCH, P])
    BN = at("BN", 77, [P, 2, 2, 3, M])
    FI = at("FI", 86, [P, 2, S])
    EG = at("EG", 74, [P, 6, S])
    YH = at("YH", 24, [P, 12, S], F32R)
    YL = at("YL", 48, [P, 12, S], F32R)
    GH = at("GH", 0, [P, KB, S], F32R)
    GL = at("GL", 72, [P, KB, S], F32R)
    FH = at("FH", 0, [P, FB, S], F32R)
    FL = at("FL", 44, [P, FB, S], F32R)
    AH = at("AH", 0, [P, KB, S], F32R)
    AL = at("AL", 16, [P, KB, S], F32R)
    FQ = at("FQ", 32, [P, 2, S])
    FK = at("FK", 36, [P, 2, S])
    FV = at("FV", 40, [P, 2, TB, P])
    FG = at("FG", 44, [P, 2, S])
    FX = at("FX", 48, [P, 2, S])
    FP = at("FP", 52, [P, 2, S])
    CB = at("CB", 56, [P, 2, 2, S])
    FY = at("FY", 64, [P, KB, S])
    FC = at("FC", 80, [16, 3, S])
    NMR = at("NMR", 86, [P, 2, P], F32R)
    IDR = at("IDR", 87, [P, P], F32R)

    UE_AT = (0, 3, 2, 1)
    bank = [nc.alloc_psum_tensor(f"bank{b}", [P, S], F32) for b in range(8)]
    LB = bank[0:2]
    SB = bank[2:4]
    TRB = bank[4:6]
    OB = bank[6:8]
    NB = bank[7]

    gates_d = nc.dram_tensor("gates_scratch", [2, 64, S], F32, kind="Internal").ap()
    fc_d = nc.dram_tensor("forget_scratch", [16, S], F32, kind="Internal").ap()

    sem = nc.alloc_semaphore
    raw_full = [sem(f"raw_full{s}") for s in range(NSLOT)]
    hi_ready, lo_ready, unit_done = sem("hi_ready"), sem("lo_ready"), sem("unit_done")
    lin_free = sem("lin_free")
    par_ready = sem("par_ready")
    x_in, par_in, mem_in, consts, masks = [sem(f"x_in{h}") for h in range(4)], sem("par_in"), [sem(f"mem_in{h}") for h in range(2)], sem("consts"), sem("masks")
    sq_ready, split_ready = sem("sq_ready"), sem("split_ready")
    fin_sum = sem("fin_sum")
    norm_sum, r_ready = sem("norm_sum"), sem("r_ready")
    epi_done, half_act, v_src, v_ready = sem("epi_done"), sem("half_act"), sem("v_src"), sem("v_ready")
    extra_full = sem("extra_full")
    s_full, s_read, mx_ready, p_exp, p_ready = (sem(n) for n in ("s_full", "s_read", "mx_ready", "p_exp", "p_ready"))
    t_full, t_out, pv_done, o_free = sem("t_full"), sem("t_out"), sem("pv_done"), sem("o_free")
    bias_in = [sem("bias_in0"), sem("bias_in1")]
    bias_ready = sem("bias_ready")
    gate_dve, gate_act, gates_out, ue_in = sem("gate_dve"), sem("gate_act"), sem("gates_out"), sem("ue_in")
    e_arg, e_ready, ms_full, ms_read, mp_ready, mpv_done, nd_free = (
        sem(n) for n in ("e_arg", "e_ready", "ms_full", "ms_read", "mp_ready", "mpv_done", "nd_free"))
    h_ready, h_sq, h_sum, h_rs, y_arg, y_done = (sem(n) for n in ("h_ready", "h_sq", "h_sum", "h_rs", "y_arg", "y_done"))
    yh_ready, yl_ready = sem("yh_ready"), sem("yl_ready")
    mg_arg, mg_act, mrg, mrg_hi, mrg_lo = (sem(n) for n in ("mg_arg", "mg_act", "mrg", "mrg_hi", "mrg_lo"))
    conv_ready, glu_ready, ff_ready, ffh_ready, ffl_ready = (
        sem(n) for n in ("conv_ready", "glu_ready", "ff_ready", "ffh_ready", "ffl_ready"))
    a_ready, ah_ready, al_ready = sem("a_ready"), sem("ah_ready"), sem("al_ready")
    fgate_dve, fgate_act, fc_out = sem("fgate_dve"), sem("fgate_act"), sem("fc_out")
    cb_in = [sem("cb_in0"), sem("cb_in1")]
    q_raw, q_sq, q_sum, q_ms, q_rs, fg_ready = (
        sem(n) for n in ("q_raw", "q_sq", "q_sum", "q_ms", "q_rs", "fg_ready"))
    f_src, f_trs, f_v, f_g, f_th, f_epi = (sem(n) for n in ("f_src", "f_trs", "f_v", "f_g", "f_th", "f_epi"))
    fs_full, fs_read, fmx, fp_exp, fp_ready, ft_full, ft_out, fpv, fo_free, fy = (
        sem(n) for n in ("fs_full", "fs_read", "fmx", "fp_exp", "fp_ready", "ft_full", "ft_out", "fpv", "fo_free",
                         "fy"))
    mask_ready = sem("mask_ready")
    oh_ready, ol_ready = sem("oh_ready"), sem("ol_ready")
    out_done = sem("out_done")

    def col(name, n=0, rows=slice(0, P)):
        return PAR[rows, bass.ds(COL[name] + n, 1)]

    def blk(t, n):
        return t[:, bass.ds(n, 1), :].rearrange("p o s -> p (o s)")

    block = nc.Block()
    block.__enter__()

    @block.sync
    def _(sp):
        def load(u0, j, i, per, src, width):
            s = (u0 + j) % NSLOT
            if u0 + j >= NSLOT:
                sp.wait_ge(lo_ready, i * per + (u0 + j - NSLOT + 1))
            sp.dma_start(RAW[:, s, 0:width], src).then_inc(raw_full[s], 16)

        def stream(name, w, iters, per):
            with sp.Fori(0, iters) as i:
                for j in range(per):
                    load(U[name], j, i, per, w[bass.ds(i * per + j, 1), :, :].rearrange("o p n -> p (o n)"), UW)

        def stream_down(name, w):
            with sp.Fori(0, 2) as i:
                for j in range(12):
                    k0 = sum(DOWN_KC[:j % 3]) * P
                    kw = DOWN_KC[j % 3] * P
                    load(U[name], j, i, 12,
                         w[bass.ds(i * 4 + j // 3, 1), :, k0:k0 + kw].rearrange("o p n -> p (o n)"), kw)

        sp.dma_start(PAR[:], A["par"]).then_inc(par_in, 16)
        sp.dma_start(MEMT[:, 0:KB // 2, :], A["mem"][:, 0:KB // 2, :]).then_inc(mem_in[0], 16)
        for u in range(NATT):
            wd = UW // 2 if UNITS[u][0] == "br" else UW
            load(0, u, 0, 0, A["w_att"][u, :, 0:wd], wd)
            if u == 0:
                sp.dma_start(MEMT[:, KB // 2:KB, :], A["mem"][:, KB // 2:KB, :]).then_inc(mem_in[1], 16)
            if u < 4:
                sp.dma_start(X[:, 2 * u:2 * u + 2, :], A["x"][:, 2 * u:2 * u + 2, :]).then_inc(x_in[u], 16)
            if UNITS[u] in BIAS_AFTER:
                p = BIAS_AFTER[UNITS[u]]
                if p == 0:
                    sp.wait_ge(unit_done, 8)
                if p >= 2:
                    sp.wait_ge(s_read, 2 * (SIDX[("na", p - 2, 3)] + 1))
                sp.dma_start(BN[:, p % 2, :, :, :], A["rpb"][p, :, :, :, :]).then_inc(bias_in[p % 2], 16)
            heads = {("mlq", 1): (0,), ("mlq", 2): (1, 2, 3)}.get(UNITS[u], ())
            if heads:
                sp.wait_ge(gates_out, 32)
                if heads[0] == 0:
                    sp.wait_ge(v_ready, VEV[("gate", 0)] + 1)
                else:
                    sp.wait_ge(o_free, 2 + 4)
                for h in heads:
                    for g in range(2):
                        for d in range(2):
                            row = gates_d[g, 32 * d + h, :]
                            sp.dma_start(UE[:, UE_AT[h], 2 * g + d, :], row.partition_broadcast(P)).then_inc(ue_in, 16)
        for j in range(4):
            n, b = (j + 2) // 3, (j + 2) % 3
            c0 = 3 * UW + b * (UW // 2)
            load(U["merge"], j, 0, 0, A["w_mrg"][n, :, c0:c0 + UW // 2], UW // 2)
        with sp.Fori(1, 4) as i:
            for j in range(12):
                n, r = j // 6, j % 6
                wd = UW if r < 3 else UW // 2
                c0 = r * UW if r < 3 else 3 * UW + (r - 3) * wd
                load(UM, j, i, 12,
                     A["w_mrg"][bass.ds(i * 2 + n, 1), :, c0:c0 + wd].rearrange("o p n -> p (o n)"), wd)
        stream("out", A["w_out"], 2, 4)
        stream("up0", A["w_up0"], 11, 4)
        stream_down("down0", A["w_down0"])
        stream("ain", A["w_ain"], 6, 4)
        stream("aout", A["w_aout"], 2, 4)
        stream("up1", A["w_up1"], 11, 4)
        stream_down("down1", A["w_down1"])
        load(U["f"], 0, 0, 0, A["w_f"], UW)
        for p in range(FA_PAIRS + 1):
            for j in range(4):
                if p < FA_PAIRS:
                    load(U["fa"], 4 * p + j, 0, 0, A["w_fa"][4 * p + j, :, :], UW)
                if p >= 1 and j == 2:
                    pp = p - 1
                    if pp == 0:
                        sp.wait_ge(fc_out, 16)
                    if pp >= 2:
                        sp.wait_ge(fs_read, 8 * (pp - 1))
                    for h in range(2):
                        sp.dma_start(CB[:, pp % 2, h, :], fc_d[2 * pp + h, :].partition_broadcast(P))\
                            .then_inc(cb_in[pp % 2], 16)
        stream("bout", A["w_bout"], 2, 4)
        stream("up2", A["w_up2"], 11, 4)
        stream_down("down2", A["w_down2"])
        for n in range(KB):
            sp.wait_ge(lin_free, O["down2"] + n + 3)
            sp.dma_start(out[n, :, :], X[:, n, :]).then_inc(out_done, 16)
        sp.wait_ge(out_done, 16 * KB)

    @block.gpsimd
    def _(pool):
        def lo(u0, j, i, per):
            s = (u0 + j) % NSLOT
            pool.wait_ge(hi_ready, i * per + (u0 + j + 1))
            nc.gpsimd.tensor_tensor(WL[:, s, :], RAW[:, s, :], WH[:, s, :].bitcast(F32), ALU.subtract)\
                .then_inc(lo_ready, 1)

        def los(name, iters, per):
            with pool.Fori(0, iters) as i:
                for j in range(per):
                    lo(U[name], j, i, per)

        for t, v in ((ONES, 1.0), (BLK, 0.0), (IDN, 0.0), (LO, 1.0), (UP, 1.0), (NM, 0.0), (EPSC, EPS), (ZERO, 0.0)):
            nc.gpsimd.memset(t[:], v).then_inc(consts, 1)
        pool.wait_ge(consts, 8)
        nc.gpsimd.memset(EPSC[:, 1:2], EPS * EPS)
        nc.gpsimd.memset(BLK[0:64, 0:64], 1.0)
        pool.drain()
        nc.gpsimd.memset(BLK[64:128, 64:128], 1.0)
        pool.drain()
        nc.gpsimd.affine_select(out=IDN[:], in_=IDN[:], compare_op=ALU.not_equal, fill=1.0, base=0,
                                pattern=[[-1, P]], channel_multiplier=1)
        nc.gpsimd.affine_select(out=LO[:], in_=LO[:], compare_op=ALU.is_ge, fill=0.0, base=0,
                                pattern=[[1, P]], channel_multiplier=-1)
        nc.gpsimd.affine_select(out=UP[:], in_=UP[:], compare_op=ALU.is_ge, fill=0.0, base=0,
                                pattern=[[-1, P]], channel_multiplier=1)
        for half in range(2):
            r = slice(64 * half, 64 * half + 64)
            pool.drain()
            nc.gpsimd.affine_select(out=NM[r], in_=NM[r], compare_op=ALU.is_ge, fill=NEG, base=0,
                                    pattern=[[-64, 2], [1, P]], channel_multiplier=-1)
        pool.drain().then_inc(masks, 1)
        for u in range(NATT):
            lo(0, u, 0, 0)
            if UNITS[u] in BIAS_AFTER:
                p = BIAS_AFTER[UNITS[u]]
                pool.wait_ge(bias_in[p % 2], 16 * (p // 2 + 1))
                def select(first, count, base, step):
                    for j in range(2):
                        r = BN[:, p % 2, j, v, ROWS * first:ROWS * (first + count)].rearrange(
                            "p (c r) -> p c r", r=ROWS)
                        last = nc.gpsimd.affine_select(
                            out=r, in_=r, compare_op=ALU.is_ge, fill=NEG, base=base + step * ROWS * first,
                            pattern=[[step * ROWS, count], [0, ROWS]], channel_multiplier=-step)
                    return last

                for v in range(3):
                    select(0, 8 if v == 0 else 16, ROWS * (8 - 8 * v) + ROWS - 1, 1)
                pool.drain()
                for v in range(3):
                    first = 24 if v == 2 else 16
                    last = select(first, KC - first, ROWS * (7 + 8 * v), -1)
                last.then_inc(bias_ready, 1)
                pool.drain()
            if UNITS[u] == ("br", 0):
                for n in range(8):
                    pool.wait_ge(yh_ready, n + 1)
                    nc.gpsimd.tensor_tensor(YL[:, n, :], Y[:, n, :], YH[:, n, :].bitcast(F32), ALU.subtract)\
                        .then_inc(yl_ready, 1)
        for j in range(4):
            lo(U["merge"], j, 0, 0)
        with pool.Fori(1, 4) as i:
            for j in range(12):
                lo(UM, j, i, 12)
        los("out", 2, 4)
        los("up0", 11, 4)
        los("down0", 2, 12)
        los("ain", 6, 4)
        los("aout", 2, 4)
        los("up1", 11, 4)
        los("down1", 2, 12)
        lo(U["f"], 0, 0, 0)
        los("fa", 8, 4)
        los("bout", 2, 4)
        los("up2", 11, 4)
        los("down2", 2, 12)

    @block.scalar
    def _(act):
        A_ = nc.scalar.activation

        def hi(u0, j, i, per):
            if not isinstance(i, int) or u0 + j + i * per < NUNITS:
                s = (u0 + j) % NSLOT
                act.wait_ge(raw_full[s], i * (16 * per // NSLOT) + 16 * ((u0 + j) // NSLOT + 1))
                if u0 + j >= NSLOT:
                    act.wait_ge(unit_done, i * per + (u0 + j - NSLOT + 1))
                A_(WH[:, s, :], RAW[:, s, :], ACT.Copy).then_inc(hi_ready, 1)

        AHEAD = 3
        LN_EXP = "natural_log_exp_and_others"

        def split(src, n, name, g, dst, width=S):
            c = SPL[name] + n
            if c >= 2:
                act.wait_ge(split_ready, c - 1)
            A_((SQ, TE)[c % 2][:, 0:width], src, ACT.Square)
            A_(dst, src, ACT.Identity, scale=g).then_inc(sq_ready, 1)

        def rstd(name, dst, width, inv):
            if name != "down0":
                act.preload_act_table_set(LN_EXP)
            act.wait_ge(norm_sum, NORM[name] + 1)
            A_(TE[:, 0:width], NB[:, 0:width], ACT.Ln, scale=inv, bias=EPSC[:, 0:1])
            act.drain()
            A_(dst, TE[:, 0:width], ACT.Exp, scale=-0.5).then_inc(r_ready, 1)

        act.preload_act_table_set(LN_EXP)
        act.wait_ge(par_in, 16)
        for n in range(KB):
            if n % 4 == 0:
                act.wait_ge(mem_in[n // 4], 16)
            split(MEMT[:, n, :], n, "mem", col("mem_g", n), MH[:, n, :], M)
            if n == 2:
                hi(0, 0, 0, 0)

        def x_split(n):
            if n % 2 == 0:
                act.wait_ge(x_in[n // 2], 16)
            split(X[:, n, :], n, "x", col("mix_g", n), XH[:, n, :])

        for n in range(1, AHEAD):
            hi(0, n, 0, 0)
        act.wait_ge(masks, 1)
        rstd("mem", RM[:], M, 1.0 / D)
        act.drain()
        x_split(0)
        x_split(1)

        for t, (un, st) in enumerate(SLOTS):
            u = UIDX[un] if un else None
            if un:
                hi(0, u + AHEAD, 0, 0)
            if t < 6:
                x_split(t + 2)
            if un == ("xq", 0):
                act.drain()
                rstd("x", R[:], S, 1.0 / D)
                act.wait_ge(par_ready, 1)
                A_(GE[:], GE[:], ACT.Ln, bias=EPSC[:, 0:1])
                act.drain()
                A_(GE[:], GE[:], ACT.Exp, scale=0.5)
            if st and st[0] in ("xa", "na"):
                g = SIDX[st]
                for j in range(2):
                    act.wait_ge(mx_ready, 2 * g + j + 1)
                    A_(SX[:, j, 0:M], SX[:, j, 0:M], ACT.Exp, bias=NX[:, j:j + 1],
                       accum_out=RS[:, j:j + 1]).then_inc(p_exp, 1)
            if st and st[0] == "ml":
                m = 4 * st[1] + st[2]
                s = st[2]
                act.wait_ge(e_arg, m + 1)
                A_(SX[:, 0, P * s:S], SX[:, 0, P * s:S], ACT.Exp, scale=-1.0)
                A_(SX[:, 1, 0:P * (s + 1)], SX[:, 1, 0:P * (s + 1)], ACT.Exp, scale=-1.0).then_inc(e_ready, 1)
            if st and st[0] in ("xa", "na"):
                g = SIDX[st]
                for j in range(2):
                    act.wait_ge(t_full, 2 * g + j + 1)
                    if g >= 1:
                        act.wait_ge(pv_done, 2 * g + j - 1)
                    A_(PT[:, j, 0:M], TRB[j][:, 0:M], ACT.Copy).then_inc(t_out, 1)
            if st == ("end", 4, 0):
                act.wait_ge(nd_free, ML_H)
                for n in range(8):
                    A_(YH[:, n, :], Y[:, n, :], ACT.Copy).then_inc(yh_ready, 1)
            if finishing(st):
                h = st[1] - 1
                if 2 in finishing(st):
                    act.wait_ge(h_ready, h + 1)
                    A_(SQ[:], FI[:, 0, :], ACT.Square).then_inc(h_sq, 1)
            if un and un[0] in HALF:
                k = sum(1 for x in UNITS[:u] if x[0] in HALF)
                act.wait_ge(half_act, k + 1)
                if un[0] == "mlo":
                    A_(SO[:, un[1] % 2, :], TA[:], ACT.Tanh, scale=0.5).then_inc(y_arg, 1)
                elif un[0] == "mg":
                    q = un[1]
                    c = (2 - q % 3) * KB + q // 3
                    A_(EG[:, q, :], TA[:], ACT.Tanh, scale=0.5, bias=HB[:, c:c + 1])\
                        .then_inc(y_arg, 1)
                else:
                    A_(TA[:], TC[:], ACT.Tanh, scale=0.5).then_inc(y_arg, 1)
            if 3 in finishing(st):
                act.preload_act_table_set(LN_EXP)
                act.wait_ge(h_sum, st[1])
                A_(TD[:], TD[:], ACT.Ln, scale=1.0 / P, bias=EPSC[:, 0:1])
                act.drain()
                A_(TD[:], TD[:], ACT.Exp, scale=-0.5).then_inc(h_rs, 1)
            if t == GATE_T + 1:
                act.wait_ge(gate_dve, 1)
                A_(GT[:, 2, :], GT[:, 2, :], ACT.Abs)
                act.drain()
                A_(GT[:, 2, :], GT[:, 2, :], ACT.Exp, scale=-1.0)
                act.drain()
                A_(GT[:, 2, :], GT[:, 2, :], ACT.Ln, bias=ONES[0:64, 0:1]).then_inc(gate_act, 1)
            if t == GATE_T + 4:
                act.wait_ge(gate_dve, 2)
                A_(GU[:, 1, :], GU[:, 1, :], ACT.Exp, scale=-1.0).then_inc(gate_act, 1)
                act.wait_ge(gate_act, 2)
                act.dma_start(gates_d[0, :, :], GU[:, 0, :]).then_inc(gates_out, 16)
                act.dma_start(gates_d[1, :, :], GU[:, 1, :]).then_inc(gates_out, 16)
            if st == ("end", 4, 3):
                act.wait_ge(y_done, ML_H)
                for n in range(8, 12):
                    A_(YH[:, n, :], Y[:, n, :], ACT.Copy).then_inc(yh_ready, 1)
        def merged_hi(i, n):
            act.wait_ge(mrg, i * 2 + (n + 1))
            A_(blk(GH, i * 2 + n), TA[:], ACT.Copy).then_inc(mrg_hi, 1)

        for j in range(4):
            hi(U["merge"], j + AHEAD, 0, 0)
            if j % 3 == 0:
                merged_hi(0, j // 3)
        with act.Fori(1, 4) as i:
            for n in range(2):
                for b in range(3):
                    hi(UM, 6 * n + b + AHEAD, i, 12)
                    act.wait_ge(mg_arg, i * 6 + (3 * n + b - 5))
                    A_(TC[:] if b == 0 else TD[:] if b == 1 else TE[:], TA[:], ACT.Tanh, scale=0.5,
                       bias=HB[:, bass.ds(i * 2 + ((2 - b) * KB + n), 1)]).then_inc(mg_act, 1)
                for b in range(3):
                    hi(UM, 6 * n + 3 + b + AHEAD, i, 12)
                merged_hi(i, n)

        def residual(name, iters, per, outs, gain, last=False):
            def body(i, at_end):
                for j in range(per):
                    if not (at_end and j + AHEAD >= per):
                        hi(U[name], j + AHEAD, i, per)
                    if (j + 1) % (per // outs) == 0:
                        n = j // (per // outs)
                        nn = i * outs + n
                        if not last:
                            act.wait_ge(lin_free, i * outs + (O[name] + n + 3))
                            act.wait_ge(split_ready, i * outs + (SPL[name] + n))
                            A_(blk(XH, nn), blk(X, nn), ACT.Identity, scale=col(gain, nn))
                            if name == "down0":
                                A_(TE[:], blk(X, nn), ACT.Square, scale=GE[:, bass.ds(nn, 1)])
                            A_(SQ[:], blk(X, nn), ACT.Square).then_inc(sq_ready, 1)
            if last:
                body(0, False)
                body(1, True)
            else:
                with act.Fori(0, iters) as i:
                    body(i, False)
                act.wait_ge(split_ready, SPL[name] + KB)
                if name == "down0":
                    act.preload_act_table_set(LN_EXP)
                    act.wait_ge(fin_sum, 1)
                    A_(TD[:], bank[6][:], ACT.Ln, scale=1.0 / D, bias=EPSC[:, 1:2])
                    act.wait_ge(norm_sum, NORM[name] + 1)
                    act.drain()
                    A_(SS[:], TD[:], ACT.Exp, scale=-0.5)
                rstd(name, R[:], S, 1.0 / D)

        def up(name, l, iters, fn):
            with act.Fori(0, iters) as i:
                for n in range(2):
                    hi(U[name], 2 * n + AHEAD, i, 4)
                    act.wait_ge(conv_ready, i * 2 + (FB * l + n + 1))
                    A_(TD[:], TC[:], fn).then_inc(glu_ready, 1)
                    hi(U[name], 2 * n + 1 + AHEAD, i, 4)
                    act.wait_ge(ff_ready, i * 2 + (FB * l + n + 1))
                    A_(blk(FH, i * 2 + n), TA[:], ACT.Copy).then_inc(ffh_ready, 1)

        residual("out", 2, 4, 4, "fg0")
        up("up0", 0, 11, ACT.Gelu_apprx_tanh)
        residual("down0", 2, 12, 4, "ag0")
        with act.Fori(0, 2) as i:
            for n in range(4):
                for r in range(3):
                    hi(U["ain"], 3 * n + r + AHEAD, i, 12)
                act.wait_ge(a_ready, i * 4 + (n + 1))
                A_(blk(AH, i * 4 + n), TA[:], ACT.Copy).then_inc(ah_ready, 1)
        residual("aout", 2, 4, 4, "fg1")
        up("up1", 1, 11, ACT.Silu)
        residual("down1", 2, 12, 4, "kvg")
        def other_split(half):
            with act.Fori(4 * half, 4 * half + 4) as i:
                A_(blk(AH, i), blk(X, i), ACT.Identity, scale=col("ag1", i)).then_inc(ah_ready, 1)

        hi(U["f"], AHEAD, 0, 0)
        other_split(0)

        def o_split(n):
            act.wait_ge(fy, n + 1)
            if n == 0:
                act.wait_ge(unit_done, U["bout"])
            A_(AH[:, n, :], FY[:, n, :], ACT.Copy).then_inc(oh_ready, 1)

        for p in range(FA_PAIRS + 1):
            for s in range(4):
                if p < FA_PAIRS:
                    hi(U["fa"], 4 * p + s + AHEAD, 0, 0)
                if p >= 1:
                    g = 4 * (p - 1) + s
                    nk = P * (s + 1)
                    for j in range(2):
                        act.wait_ge(fmx, 2 * g + j + 1)
                        A_(FX[:, j, 0:nk], FX[:, j, 0:nk], ACT.Exp, bias=NX[:, j:j + 1],
                           accum_out=RS[:, j:j + 1]).then_inc(fp_exp, 1)
                if p < FA_PAIRS and s in (1, 2):
                    act.wait_ge(q_ms, 2 * p + s)
                    A_(TD[:], SS[:], ACT.Ln)
                    act.drain()
                    A_(TD[:], TD[:], ACT.Exp, scale=-0.5).then_inc(q_rs, 1)
                if p < FA_PAIRS and s < 2:
                    act.wait_ge(q_raw, 2 * p + s + 1)
                    A_(SQ[:], TA[:], ACT.Square).then_inc(q_sq, 1)
                if p == 0 and s == 0:
                    other_split(1)
                    A_(NMR[:], NM[:], ACT.Copy)
                    A_(IDR[:], IDN[:], ACT.Copy)
                    act.drain().then_inc(mask_ready, 1)
                if p == 0 and s == 1:
                    act.wait_ge(fgate_dve, 1)
                    A_(FC[:, 2, :], FC[:, 2, :], ACT.Abs)
                    act.drain()
                    A_(FC[:, 2, :], FC[:, 2, :], ACT.Exp, scale=-1.0)
                    act.drain()
                    A_(FC[:, 2, :], FC[:, 2, :], ACT.Ln, bias=ONES[0:16, 0:1]).then_inc(fgate_act, 1)
                if p == 0 and s == 3:
                    act.wait_ge(fgate_dve, 2)
                    act.dma_start(fc_d[:, :], FC[:, 1, :]).then_inc(fc_out, 16)
                if p < FA_PAIRS and s == 3:
                    act.wait_ge(f_g, p + 1)
                    A_(TE[:], TC[:], ACT.Exp, scale=-1.0).then_inc(f_th, 1)
                    act.drain()
                    A_(TE[:], TE[:], ACT.Ln, bias=ONES[:, 0:1])
                    act.drain()
                    A_(FG[:, p % 2, :], TE[:], ACT.Exp, scale=-1.0).then_inc(fg_ready, 1)
                if p >= 1:
                    for j in range(2):
                        act.wait_ge(ft_full, 2 * g + j + 1)
                        if g >= 1:
                            act.wait_ge(fpv, 2 * g + j - 1)
                        A_(FP[:, j, 0:nk], TRB[j][:, 0:nk], ACT.Copy).then_inc(ft_out, 1)
                if p == FA_PAIRS and s >= 1:
                    o_split(2 * s - 2)
                    o_split(2 * s - 1)
        for n in (6, 7):
            o_split(n)
        residual("bout", 2, 4, 4, "fg2")
        up("up2", 2, 11, ACT.Silu)
        residual("down2", 2, 12, 4, None, last=True)

    @block.vector
    def _(dve):
        v = nc.vector

        def split(src, n, name, g, h, l, width=S, acc=SS):
            c = SPL[name] + n
            dve.wait_ge(sq_ready, c + 1)
            v.tensor_tensor(acc[:, 0:width], acc[:, 0:width], (SQ, TE)[c % 2][:, 0:width], ALU.add)
            v.scalar_tensor_tensor(out=l, in0=src, scalar=g, in1=h.bitcast(F32), op0=ALU.mult,
                                   op1=ALU.subtract).then_inc(split_ready, 1)

        dve.sem_inc(lin_free, 2)
        v.memset(SS[:], 0.0)
        v.memset(TD[:, 0:M], 0.0)
        dve.wait_ge(par_in, 16)
        v.tensor_scalar(HB[:], PAR[:, COL["bmg"]:COL["bmg"] + 24], 0.5, None, ALU.mult)
        mlg = PAR[:, COL["mlg"]:COL["mlg"] + ML_H]
        v.tensor_scalar(mlg, mlg, 0.5, None, ALU.mult)
        ag = PAR[:, COL["ag0"]:COL["ag0"] + KB]
        fin = PAR[:, COL["fin"]:COL["fin"] + KB]
        v.tensor_tensor(ag, ag, fin, ALU.mult)
        v.tensor_tensor(GE[:], fin, fin, ALU.mult)
        v.tensor_scalar(PAR[:, COL["qn"]:COL["qn"] + 1], PAR[:, COL["qn"]:COL["qn"] + 1], 0.125, None, ALU.mult)
        dve.drain().then_inc(par_ready, 1)
        for n in range(KB):
            split(MEMT[:, n, :], n, "mem", col("mem_g", n), MH[:, n, :], ML[:, n, :], M, TD)
            dve.drain()

        def x_split(n):
            split(X[:, n, :], n, "x", col("mix_g", n), XH[:, n, :], XL[:, n, :])
            dve.drain()

        def by_rows(t, columns):
            return t.rearrange("p (c r) -> p r c" if columns else "p (r c) -> p r c", c=GRID)

        def read_lin(ev, out_, in1, scalar=None):
            b = LB[LEV[ev] % 2]
            in0 = b[:, 0:in1.shape[1]]
            if ev[0] in ("naq", "nak", "nav"):
                in0, in1, out_ = by_rows(in0, False), by_rows(in1, False), by_rows(out_, True)
            if scalar is None:
                v.tensor_tensor(out_, in0, in1, ALU.mult).then_inc(lin_free, 1)
            else:
                v.scalar_tensor_tensor(out=out_, in0=in0, scalar=scalar, in1=in1, op0=ALU.mult,
                                       op1=ALU.mult).then_inc(lin_free, 1)

        def conv3(c, taps, n, bias, off):
            mid = 0 - off
            w = [col(x, n) for x in taps]
            if bias is not None:
                v.tensor_scalar(TC[:], c[:], w[mid], col(bias, n), ALU.mult, ALU.add)
            else:
                v.tensor_scalar(TC[:], c[:], w[mid], None, ALU.mult)
            last = None
            for k in range(3):
                d = k + off
                if d == 0:
                    continue
                dve.drain()
                if d < 0:
                    last = v.scalar_tensor_tensor(out=TC[:, -d:S], in0=c[:, 0:S + d], scalar=w[k],
                                                  in1=TC[:, -d:S], op0=ALU.mult, op1=ALU.add)
                else:
                    last = v.scalar_tensor_tensor(out=TC[:, 0:S - d], in0=c[:, d:S], scalar=w[k],
                                                  in1=TC[:, 0:S - d], op0=ALU.mult, op1=ALU.add)
            return last

        def finish_head(h):
            dve.wait_ge(h_rs, h + 1)
            v.scalar_tensor_tensor(out=Y[:, 8 + h, :], in0=FI[:, 0, :], scalar=col("mlg", h), in1=TD[:],
                                   op0=ALU.mult, op1=ALU.mult).then_inc(y_done, 1)
            dve.drain()

        def branch(gates, b, bank_):
            v.scalar_tensor_tensor(out=gates[b], in0=gates[b], scalar=1.0, in1=bank_[:], op0=ALU.add, op1=ALU.mult)\
                .then_inc(lin_free, 1)
            dve.drain()
            if b == 1:
                v.tensor_tensor(gates[0], gates[0], gates[1], ALU.add)
                dve.drain()

        halfs = 0
        extras = 0
        MC = 0.25 * 128 ** -0.5
        for t, (un, st) in enumerate(SLOTS):
            if un in (("memk", 0), ("xq", 0)):
                dve.wait_ge(r_ready, 1 if un[0] == "memk" else 2)
            if st and st[0] == "ml":
                h, s = st[1], st[2]
                m = 4 * h + s
                if m % 4 == 0:
                    dve.wait_ge(ue_in, 64 * (h + 1))
                if m == 0:
                    dve.wait_ge(t_full, 2 * len(STEPS))
                v.tensor_scalar(SX[:, 0, P * s:S], UE[:, UE_AT[h], 0, P * s:S], UT[:, s, h:h + 1], 0.0,
                                ALU.subtract, ALU.max)
                v.tensor_scalar(SX[:, 1, 0:P * (s + 1)], UE[:, UE_AT[h], 1, 0:P * (s + 1)], UT[:, s, 32 + h:33 + h], 0.0,
                                ALU.subtract, ALU.max).then_inc(e_arg, 1)
                if s == 0 and h >= 2:
                    finish_head(h - 2)
            if st and st[0] in ("xa", "na"):
                g = SIDX[st]
                if st[0] == "na" and st[2] == 0:
                    dve.wait_ge(bias_ready, st[1] + 1)
                for j in range(2):
                    dve.wait_ge(s_full, 2 * g + j + 1)
                    if g >= 1:
                        dve.wait_ge(t_full, 2 * g + j - 1)
                    if st[0] == "xa":
                        b = ZERO[:]
                    else:
                        b = BN[:, st[1] % 2, j, VAR[st[2]], :]
                    v.tensor_tensor_reduce(out=SX[:, j, 0:M], in0=SB[j][:, 0:M], in1=b, scale=1.0, scalar=NEG,
                                           op0=ALU.add, op1=ALU.max, accum_out=MX[:, j:j + 1]).then_inc(s_read, 1)
                    dve.drain()
                    v.tensor_scalar(NX[:, j:j + 1], MX[:, j:j + 1], -1.0, None, ALU.mult).then_inc(mx_ready, 1)
            if st and st[2] == 0 and t > 0 and SLOTS[t - 1][1] is not None and SLOTS[t - 1][1][0] in ("xa", "na"):
                pk, pp, _ = SLOTS[t - 1][1]
                dve.wait_ge(pv_done, 2 * SIDX[(pk, pp, 3)] + 2)
                if pk == "xa":
                    v.tensor_copy(Y[:, 2 * pp, :], OB[0][:])
                    v.tensor_copy(Y[:, 2 * pp + 1, :], OB[1][:]).then_inc(o_free, 1)
                else:
                    v.tensor_copy(by_rows(Y[:, 4 + pp, :], False), by_rows(OB[0][:], True)).then_inc(o_free, 1)
            if st and st[0] in ("xa", "na"):
                for j in range(2):
                    dve.wait_ge(p_exp, 2 * g + j + 1)
                    v.reciprocal(RI[:, j:j + 1], RS[:, j:j + 1])
                    dve.drain()
                    v.tensor_scalar(SX[:, j, 0:M], SX[:, j, 0:M], RI[:, j:j + 1], None, ALU.mult)\
                        .then_inc(p_ready, 1)
            if st and st[0] == "ml":
                dve.wait_ge(e_ready, m + 1)
                dve.wait_ge(ms_full, m + 1)
                if m >= 2:
                    dve.wait_ge(mpv_done, m - 1)
                if m == 0:
                    dve.wait_ge(pv_done, 2 * len(STEPS))
                    v.memset(PB[:, 2, P:S], 0.0)
                b = SB[m % 2]
                pb = 2 if s == 0 else s % 2
                v.scalar_tensor_tensor(out=PT[:, m % 2, P * s:S], in0=b[:, P * s:S], scalar=MC,
                                       in1=SX[:, 0, P * s:S], op0=ALU.mult, op1=ALU.mult)
                v.scalar_tensor_tensor(out=PB[:, pb, 0:P * (s + 1)], in0=b[:, 0:P * (s + 1)], scalar=MC,
                                       in1=SX[:, 1, 0:P * (s + 1)], op0=ALU.mult, op1=ALU.mult).then_inc(ms_read, 1)
                dve.drain()
                dg = slice(P * s, P * (s + 1))
                v.tensor_tensor(PT[:, m % 2, dg], PT[:, m % 2, dg], LO[:], ALU.mult)
                v.tensor_tensor(PB[:, pb, dg], PB[:, pb, dg], UP[:], ALU.mult).then_inc(mp_ready, 1)
            if st == ("end", 4, 0):
                finish_head(ML_H - 2)
            if finishing(st):
                h, steps = st[1] - 1, finishing(st)
                if 0 in steps:
                    dve.wait_ge(mpv_done, 4 * h + 4)
                    v.scalar_tensor_tensor(out=FI[:, 0, :], in0=bank[5][:], scalar=-1.0, in1=UE[:, UE_AT[h], 2, :],
                                           op0=ALU.mult, op1=ALU.max)
                    v.scalar_tensor_tensor(out=FI[:, 1, :], in0=bank[7][:], scalar=-1.0, in1=UE[:, UE_AT[h], 3, :],
                                           op0=ALU.mult, op1=ALU.max)
                    dve.drain()
                    v.tensor_tensor(FI[:, 0, :], bank[5][:], FI[:, 0, :], ALU.max)
                    v.tensor_tensor(FI[:, 1, :], bank[7][:], FI[:, 1, :], ALU.max)
                    v.tensor_copy(TE[:], bank[4][:])
                    v.tensor_copy(SS[:], bank[6][:]).then_inc(nd_free, 1)
                if 1 in steps:
                    dve.drain()
                    v.reciprocal(FI[:, 0, :], FI[:, 0, :])
                if 2 in steps:
                    v.reciprocal(FI[:, 1, :], FI[:, 1, :])
                    dve.drain()
                    v.tensor_tensor(FI[:, 0, :], FI[:, 0, :], TE[:], ALU.mult)
                    v.tensor_tensor(FI[:, 1, :], FI[:, 1, :], SS[:], ALU.mult)
                    dve.drain()
                    v.tensor_tensor(FI[:, 0, :], FI[:, 0, :], FI[:, 1, :], ALU.add).then_inc(h_ready, 1)
            if 3 in finishing(st):
                dve.wait_ge(h_sq, st[1])
                v.scalar_tensor_tensor(out=FI[:, 0, :], in0=SO[:, (st[1] - 1) % 2, :], scalar=1.0,
                                       in1=FI[:, 0, :], op0=ALU.add, op1=ALU.mult)
                dve.drain()
            if un:
                kind, n = un
                dve.wait_ge(unit_done, UIDX[un] + 1)
                if EXTRA[t] and kind in ("memv", "nav", "mlq", "mlk", "mlv"):
                    dve.wait_ge(extra_full, extras + len(EXTRA[t]))
                if kind == "memk":
                    read_lin(un, MK[:, n, :], RM[:])
                elif kind == "xq":
                    read_lin(un, XQ[:, n, :], R[:], 128 ** -0.5)
                elif kind == "naq":
                    read_lin(un, QN[:, n % 2, :], R[:], 0.125)
                elif kind == "nak":
                    read_lin(un, KN[:, n % 2, :], R[:])
                elif kind in ("memv", "nav", "mlv"):
                    w = M if kind == "memv" else S
                    read_lin(un, TC[:, 0:w], RM[:] if kind == "memv" else R[:])
                    dve.drain().then_inc(v_src, 1)
                elif kind == "gate":
                    read_lin(un, TA[:], R[:])
                    dve.drain()
                    v.tensor_scalar(GT[:, 0, :], TA[0:64, :], col("gb", 0, slice(0, 64)), None, ALU.add)
                    v.tensor_scalar(TA[64:128, :], TA[64:128, :], col("gb", 0, slice(64, 128)), None, ALU.add)
                    dve.drain()
                    v.tensor_scalar(GT[:, 1, :], TA[64:128, :], 0.0, None, ALU.min)
                    v.tensor_copy(GT[:, 2, :], TA[64:128, :]).then_inc(gate_dve, 1)
                elif kind in ("mlq", "mlk"):
                    read_lin(un, TA[:], R[:])
                    dve.drain()
                    c = n if kind == "mlq" else 4 + n
                    conv3(TA, ("mlc0", "mlc1", "mlc2"), c, "mlb", -1).then_inc(half_act, 1)
                    halfs += 1
                    dve.wait_ge(y_arg, halfs)
                    v.scalar_tensor_tensor(out=(Q if kind == "mlq" else K)[:, n % 2, :], in0=TA[:], scalar=1.0,
                                           in1=TC[:], op0=ALU.add, op1=ALU.mult)
                elif kind == "br":
                    branch([EG[:, c, :] for c in range(3)], n, LB[LEV[un] % 2])
                elif kind in ("mlo", "mg"):
                    read_lin(un, TA[:], R[:])
                    dve.drain().then_inc(half_act, 1)
                    halfs += 1
                    dve.wait_ge(y_arg, halfs)
                dve.drain().then_inc(epi_done, 1)
            if t < 6:
                for n in ((0, 1, 2) if t == 0 else (t + 2,)):
                    x_split(n)
            if t == GATE_T + 2:
                dve.wait_ge(gate_act, 1)
                v.tensor_tensor(GT[:, 1, :], GT[:, 1, :], GT[:, 2, :], ALU.subtract)
                v.memset(TE[0:64, :], 1.0)
                dve.drain()
                v.tensor_tensor_scan(GT[0:32, 2, :], TE[0:32, :], GT[0:32, 1, :], 0.0, ALU.mult, ALU.add)
                v.tensor_tensor_scan(GT[32:64, 2, ::-1], TE[32:64, :], GT[32:64, 1, ::-1], 0.0, ALU.mult,
                                     ALU.add)
            if t == GATE_T + 3:
                v.tensor_tensor(GT[:, 3, :], GT[:, 0, :], GT[:, 2, :], ALU.subtract)
                dve.drain()
                v.tensor_tensor_scan(GU[0:32, 0, :], GT[0:32, 3, :], GT[0:32, 3, :], NEG, ALU.max, ALU.max)
                v.tensor_tensor_scan(GU[32:64, 0, ::-1], GT[32:64, 3, ::-1], GT[32:64, 3, ::-1], NEG, ALU.max,
                                     ALU.max)
                dve.drain()
                v.tensor_tensor(GU[:, 1, :], GT[:, 2, :], GU[:, 0, :], ALU.add).then_inc(gate_dve, 1)
                dve.drain().then_inc(v_src, 1)
            for e in EXTRA[t]:
                extras += 1
                dve.wait_ge(extra_full, extras)
                b = LB[LEV[e] % 2]
                if e[0] == "hn":
                    v.tensor_copy(TD[:], b[:]).then_inc(lin_free, 1)
                    dve.drain().then_inc(h_sum, 1)
                    continue
                kind, n = e[1:]
                if kind == "memv":
                    d, w = MV[:, :, n * P:(n + 1) * P], M
                elif kind == "nav":
                    d, w = VN[:, n % 2, 0:VCH:2, :], S
                elif kind == "nav64":
                    d, w = VN[:, n % 2, 1:VCH:2, :], S - P
                elif kind == "mlv":
                    d, w = V[:, n % 2, :, :], S
                else:
                    d, w = UT[:], 4 * 64
                v.tensor_copy(d, b[:, 0:w].rearrange("p (t c) -> p t c", c=d.shape[2])).then_inc(lin_free, 1)
                dve.drain().then_inc(v_ready, 1)
            if st == ("end", 4, 3):
                finish_head(ML_H - 1)
            if st and st[0] == "end":
                for n in range(8, 12) if st[2] == 3 else ():
                    dve.wait_ge(yh_ready, n + 1)
                    v.tensor_tensor(YL[:, n, :], Y[:, n, :], YH[:, n, :].bitcast(F32), ALU.subtract)\
                        .then_inc(mrg_lo, 1)
        def merged(i, n, gates):
            v.tensor_tensor(gates[0], gates[0], gates[2], ALU.add)
            dve.drain()
            v.tensor_scalar(TA[:], gates[0], 0.5, None, ALU.mult).then_inc(mrg, 1)
            dve.wait_ge(mrg_hi, i * 2 + (n + 1))
            v.tensor_tensor(blk(GL, i * 2 + n), TA[:], blk(GH, i * 2 + n).bitcast(F32), ALU.subtract)\
                .then_inc(mrg_lo, 1)
            dve.drain()

        for j in range(4):
            n, b = (j + 2) // 3, (j + 2) % 3
            gates = [EG[:, 3 * n + c, :] for c in range(3)]
            dve.wait_ge(unit_done, U["merge"] + j + 1)
            branch(gates, b, LB[(O["merge"] + j) % 2])
            if b == 2:
                merged(0, n, gates)
        with dve.Fori(1, 4) as i:
            for n in range(2):
                for b in range(3):
                    j = 6 * n + b
                    dve.wait_ge(unit_done, i * 12 + (UM + j + 1))
                    v.tensor_tensor(TA[:], LB[(OM + j) % 2][:], R[:], ALU.mult).then_inc(lin_free, 1)
                    dve.drain().then_inc(mg_arg, 1)
                    dve.wait_ge(mg_act, i * 6 + (3 * n + b - 5))
                for b in range(3):
                    j = 6 * n + 3 + b
                    dve.wait_ge(unit_done, i * 12 + (UM + j + 1))
                    branch((TC[:], TD[:], TE[:]), b, LB[(OM + j) % 2])
                merged(i, n, (TC[:], TD[:], TE[:]))

        def residual(name, iters, per, outs, gain, last=False):
            v.memset(SS[:], 0.0)
            if name == "down0":
                v.memset(TC[:], 0.0)
            dve.drain()
            with dve.Fori(0, iters) as i:
                for n in range(outs):
                    nn = i * outs + n
                    dve.wait_ge(unit_done, i * per + (U[name] + (n + 1) * per // outs))
                    v.tensor_tensor(blk(X, nn), blk(X, nn), LB[(O[name] + n) % 2][:], ALU.add).then_inc(lin_free, 1)
                    if not last:
                        dve.drain()
                        dve.wait_ge(sq_ready, i * outs + (SPL[name] + n + 1))
                        v.tensor_tensor(SS[:], SS[:], SQ[:], ALU.add)
                        if name == "down0":
                            v.tensor_tensor(TC[:], TC[:], TE[:], ALU.add)
                        v.scalar_tensor_tensor(out=blk(XL, nn), in0=blk(X, nn), scalar=col(gain, nn),
                                               in1=blk(XH, nn).bitcast(F32), op0=ALU.mult, op1=ALU.subtract)\
                            .then_inc(split_ready, 1)
            if not last:
                dve.wait_ge(r_ready, NORM[name] + 1)

        def up(name, l, iters, off, taps, bias):
            with dve.Fori(0, iters) as i:
                for n in range(2):
                    nn = i * 2 + n
                    dve.wait_ge(unit_done, i * 4 + (U[name] + 2 * n + 1))
                    v.tensor_tensor(TA[:], LB[0 if (O[name] % 2) == 0 else 1][:], R[:], ALU.mult)\
                        .then_inc(lin_free, 1)
                    dve.drain()
                    conv3(TA, taps, nn, bias, off).then_inc(conv_ready, 1)
                    dve.wait_ge(unit_done, i * 4 + (U[name] + 2 * n + 2))
                    v.tensor_tensor(TE[:], LB[1 if (O[name] % 2) == 0 else 0][:], R[:], ALU.mult)\
                        .then_inc(lin_free, 1)
                    dve.drain()
                    dve.wait_ge(glu_ready, i * 2 + (FB * l + n + 1))
                    v.tensor_tensor(TA[:], TE[:], TD[:], ALU.mult).then_inc(ff_ready, 1)
                    dve.wait_ge(ffh_ready, i * 2 + (FB * l + n + 1))
                    v.tensor_tensor(blk(FL, nn), TA[:], blk(FH, nn).bitcast(F32), ALU.subtract).then_inc(ffl_ready, 1)
                    dve.drain()

        residual("out", 2, 4, 4, "fg0")
        up("up0", 0, 11, -1, ("fc00", "fc01", "fc02"), "fb0")
        residual("down0", 2, 12, 4, "ag0")
        with dve.Fori(0, 2) as i:
            for n in range(4):
                for r, dst in enumerate((TE, TD, TA)):
                    j = 3 * n + r
                    dve.wait_ge(unit_done, i * 12 + (U["ain"] + j + 1))
                    v.tensor_tensor(dst[:], LB[(O["ain"] + j) % 2][:], SS[:], ALU.mult).then_inc(lin_free, 1)
                v.scalar_tensor_tensor(out=blk(X, i * 4 + n), in0=blk(X, i * 4 + n), scalar=col("fin", i * 4 + n),
                                       in1=R[:], op0=ALU.mult, op1=ALU.mult)
                dve.drain()
                v.tensor_tensor(TA[:], TA[:], TD[:], ALU.mult)
                dve.drain()
                conv3(TA, ("ac0", "ac1", "ac2"), i * 4 + n, None, -2)
                dve.drain()
                v.tensor_tensor(TA[:], TC[:], TE[:], ALU.mult).then_inc(a_ready, 1)
                dve.wait_ge(ah_ready, i * 4 + (n + 1))
                v.tensor_tensor(blk(AL, i * 4 + n), TA[:], blk(AH, i * 4 + n).bitcast(F32), ALU.subtract)\
                    .then_inc(al_ready, 1)
                dve.drain()
        residual("aout", 2, 4, 4, "fg1")
        up("up1", 1, 11, -2, ("fc10", "fc11", "fc12"), None)
        residual("down1", 2, 12, 4, "kvg")
        v.memset(TE[0:16, :], 1.0)
        dve.wait_ge(unit_done, U["f"] + 1)
        v.tensor_tensor(FC[:, 1, :], LB[O["f"] % 2][0:16, :], R[0:16, :], ALU.mult).then_inc(lin_free, 1)

        def other_split(half):
            with dve.Fori(4 * half, 4 * half + 4) as i:
                dve.wait_ge(ah_ready, i + (KB + 1))
                v.scalar_tensor_tensor(out=blk(AL, i), in0=blk(X, i), scalar=col("ag1", i),
                                       in1=blk(AH, i).bitcast(F32), op0=ALU.mult, op1=ALU.subtract)\
                    .then_inc(al_ready, 1)

        other_split(0)

        def o_split(n):
            dve.wait_ge(oh_ready, n + 1)
            v.tensor_tensor(AL[:, n, :], FY[:, n, :], AH[:, n, :].bitcast(F32), ALU.subtract).then_inc(ol_ready, 1)

        def o_gate(pp):
            dve.wait_ge(fpv, 8 * (pp + 1))
            dve.wait_ge(fg_ready, pp + 1)
            v.tensor_tensor(FY[:, pp, :], OB[0][:], FG[:, pp % 2, :], ALU.mult).then_inc(fo_free, 1)
            dve.drain().then_inc(fy, 1)

        for p in range(FA_PAIRS + 1):
            o0 = O["fa"] + FA_L * p
            for s in range(4):
                if p >= 1:
                    pp = p - 1
                    g = 4 * pp + s
                    nk = P * (s + 1)
                    if s == 0:
                        dve.wait_ge(cb_in[pp % 2], 32 * (pp // 2 + 1))
                    for j in range(2):
                        dve.wait_ge(fs_full, 2 * g + j + 1)
                        if g >= 1:
                            dve.wait_ge(ft_full, 2 * g + j - 1)
                        v.tensor_tensor_reduce(out=FX[:, j, 0:nk], in0=SB[j][:, 0:nk], in1=CB[:, pp % 2, j, 0:nk],
                                               scale=1.0, scalar=NEG, op0=ALU.add, op1=ALU.max,
                                               accum_out=MX[:, j:j + 1]).then_inc(fs_read, 1)
                        dve.drain()
                        v.tensor_scalar(NX[:, j:j + 1], MX[:, j:j + 1], -1.0, None, ALU.mult).then_inc(fmx, 1)
                    for j in range(2):
                        dve.wait_ge(fp_exp, 2 * g + j + 1)
                        v.reciprocal(RI[:, j:j + 1], RS[:, j:j + 1])
                        dve.drain()
                        v.tensor_scalar(FX[:, j, 0:nk], FX[:, j, 0:nk], RI[:, j:j + 1], None, ALU.mult)\
                            .then_inc(fp_ready, 1)
                if p < FA_PAIRS:
                    if s in (1, 2):
                        dve.wait_ge(q_sum, 2 * p + s)
                        v.tensor_scalar(SS[:], LB[(o0 + (1, 3)[s - 1]) % 2][:], 1.0 / 64, EPSC[:, 0:1], ALU.mult,
                                        ALU.add).then_inc(lin_free, 1)
                        dve.drain().then_inc(q_ms, 1)
                        dve.wait_ge(q_rs, 2 * p + s)
                        v.tensor_tensor(SS[:], SS[:], TD[:], ALU.mult)
                        v.scalar_tensor_tensor(out=TA[:], in0=TA[:], scalar=col("kn" if s == 1 else "qn"),
                                               in1=TD[:], op0=ALU.mult, op1=ALU.mult)
                        dve.drain()
                        v.tensor_tensor(SS[:], SS[:], TD[:], ALU.mult)
                        dve.drain()
                        v.tensor_scalar(SS[:], SS[:], -0.5, 1.5, ALU.mult, ALU.add)
                        dve.drain()
                        v.tensor_tensor((FK if s == 1 else FQ)[:, p % 2, :], TA[:], SS[:], ALU.mult)\
                            .then_inc(f_epi, 1)
                        dve.drain()
                    if s == 3:
                        dve.wait_ge(f_trs, p + 1)
                        v.tensor_copy(FV[:, p % 2, :, :], LB[(o0 + 5) % 2][:].rearrange("p (t c) -> p t c", c=P))\
                            .then_inc(lin_free, 1)
                        dve.drain().then_inc(f_v, 1)
                    dve.wait_ge(unit_done, U["fa"] + 4 * p + s + 1)
                    b = LB[(o0 + (0, 2, 4, 6)[s]) % 2]
                    if s < 2:
                        v.tensor_tensor(TA[:], b[:], R[:], ALU.mult).then_inc(lin_free, 1)
                        dve.drain().then_inc(q_raw, 1)
                        if p == 0 and s == 0:
                            other_split(1)
                        if p == 0 and s == 1:
                            v.tensor_scalar(FC[:, 1, :], FC[:, 1, :], col("bf", 0, slice(0, 16)), None, ALU.add)
                            dve.drain()
                            v.tensor_scalar(FC[:, 0, :], FC[:, 1, :], 0.0, None, ALU.min)
                            v.tensor_copy(FC[:, 2, :], FC[:, 1, :]).then_inc(fgate_dve, 1)
                    elif s == 2:
                        if p:
                            dve.wait_ge(f_th, p)
                        v.tensor_tensor(TC[:], b[:], R[:], ALU.mult).then_inc(lin_free, 1)
                        dve.drain().then_inc(f_src, 1)
                        if p == 0:
                            dve.wait_ge(fgate_act, 1)
                            v.tensor_tensor(FC[:, 0, :], FC[:, 2, :], FC[:, 0, :], ALU.subtract)
                            dve.drain()
                            v.tensor_tensor_scan(FC[:, 1, :], TE[0:16, :], FC[:, 0, :], 0.0, ALU.mult, ALU.add)\
                                .then_inc(fgate_dve, 1)
                    else:
                        v.tensor_tensor(TC[:], b[:], R[:], ALU.mult).then_inc(lin_free, 1)
                        dve.drain()
                        v.tensor_scalar(TC[:], TC[:], -87.0, None, ALU.max)
                        dve.drain().then_inc(f_g, 1)
                if p >= 2 and s == 0:
                    o_gate(p - 2)
                if p == FA_PAIRS and s >= 1:
                    o_split(2 * s - 2)
                    o_split(2 * s - 1)
        o_split(6)
        o_gate(7)
        o_split(7)
        residual("bout", 2, 4, 4, "fg2")
        up("up2", 2, 11, -2, ("fc20", "fc21", "fc22"), None)
        residual("down2", 2, 12, 4, None, last=True)

    @block.tensor
    def _(pe):
        mm = nc.tensor.matmul

        def unit(u0, j, i, per, kc, xh, xl, k0, dst, start=True, stop=True, width=S, ready=None, before_last=None):
            s = (u0 + j) % NSLOT
            pe.wait_ge(lo_ready, i * per + (u0 + j + 1))
            for k in range(kc):
                if before_last and k == kc - 1:
                    before_last()
                if ready:
                    pe.wait_ge(ready[0], ready[1] + k + 1)
                w = slice(k * P, (k + 1) * P)
                a, b = xh[:, k0 + k, 0:width], xl[:, k0 + k, 0:width]
                mm(dst[:, 0:width], WH[:, s, w], a, start=start and k == 0, stop=False)
                mm(dst[:, 0:width], WH[:, s, w], b, start=False, stop=False)
                last = mm(dst[:, 0:width], WL[:, s, w], a, start=False, stop=stop and k == kc - 1)
            last.then_inc(unit_done, 1)

        def norm(name, src, width, total):
            pe.wait_ge(split_ready, total)
            if NORM[name]:
                pe.wait_ge(r_ready, NORM[name])
            if name == "down0":
                mm(bank[6][:], ONES[:], TC[:], start=True, stop=True).then_inc(fin_sum, 1)
            mm(NB[:, 0:width], ONES[:], src, start=True, stop=True).then_inc(norm_sum, 1)

        pe.wait_ge(consts, 8)
        pe.wait_ge(masks, 1)

        def need(un):
            pe.wait_ge(epi_done, UIDX[un] + 1)

        extras = 0

        def products(st):
            kind, p, s = st
            g = SIDX[st]
            for j in range(2):
                pe.wait_ge(t_out, 2 * g + j + 1)
                if s == 0 and j == 0:
                    pe.wait_ge(v_ready, VEV[("memv", 3)] + 1 if kind == "xa" else VEV[("nav64", p)] + 1)
                    done = p if kind == "xa" else 2 + p
                    if done:
                        pe.wait_ge(o_free, done)
                for k in range(MB):
                    if kind == "xa":
                        dst = OB[j][:, P * s:P * (s + 1)]
                        w = MV[:, k, (2 * p + j) * P:(2 * p + j + 1) * P]
                    else:
                        dst = OB[0][64 * j:64 * j + 64, P * s:P * (s + 1)]
                        w = VN[:, p % 2, KEY0[s] // 64 + 2 * k, 64 * j:64 * j + 64]
                    last = mm(dst, w, PT[:, j, k * P:(k + 1) * P], start=k == 0, stop=k == MB - 1)
                last.then_inc(pv_done, 1)

        def ml_products(h, s):
            m = 4 * h + s
            pe.wait_ge(mp_ready, m + 1)
            if s == 0:
                pe.wait_ge(v_ready, VEV[("mlv", h)] + 1)
                if h == 0:
                    pe.wait_ge(o_free, 6)
                    pe.wait_ge(t_out, 2 * len(STEPS))
                else:
                    pe.wait_ge(nd_free, h)
            fw = PT[:, m % 2, P * s:S]
            mm(bank[4][:, P * s:S], V[:, h % 2, s, :], fw, start=s == 0, stop=s == 3)
            mm(bank[5][:, P * s:S], ONES[:], fw, start=s == 0, stop=s == 3)
            w = S if s == 0 else P * (s + 1)
            bw = PB[:, 2 if s == 0 else s % 2, 0:w]
            mm(bank[6][:, 0:w], V[:, h % 2, s, :], bw, start=s == 0, stop=s == 3)
            mm(bank[7][:, 0:w], ONES[:], bw, start=s == 0, stop=s == 3).then_inc(mpv_done, 1)

        for t, (un, st) in enumerate(SLOTS):
            before = SLOTS[t - 1][1] if t else None
            if st and st[0] in ("xa", "na"):
                kind, p, s = st
                g = SIDX[st]
                if s == 0:
                    need(("xq", 2 * p + 1) if kind == "xa" else ("nak", p))
                for j in range(2):
                    if g >= 1:
                        pe.wait_ge(s_read, 2 * g + j - 1)
                    if kind == "xa":
                        h = 2 * p + j
                        mm(SB[j][:, 0:M], XQ[:, h, P * s:P * (s + 1)], MK[:, h, :], start=True, stop=True)\
                            .then_inc(s_full, 1)
                    else:
                        r = slice(64 * j, 64 * j + 64)
                        mm(SB[j][:, 0:M], QN[r, p % 2, P * s:P * (s + 1)], KN[r, p % 2, KEY0[s]:KEY0[s] + M],
                           start=True, stop=True)\
                            .then_inc(s_full, 1)
            if st and st[0] == "ml":
                _, h, s = st
                m = 4 * h + s
                if s == 0:
                    need(("mlk", h))
                if m == 0:
                    pe.wait_ge(s_read, 2 * len(STEPS))
                if m >= 2:
                    pe.wait_ge(ms_read, m - 1)
                mm(SB[m % 2][:], K[:, h % 2, P * s:P * (s + 1)], Q[:, h % 2, :], start=True, stop=True)\
                    .then_inc(ms_full, 1)
            if before and before[0] in ("xa", "na"):
                products(before)
            if before and before[0] == "ml":
                ml_products(before[1], before[2])
            if un:
                o = LEV[un]
                pe.wait_ge(lin_free, o + 1)
                if un[0] in ("memk", "memv"):
                    unit(0, UIDX[un], 0, 0, KB, MH, ML, 0, LB[o % 2], width=M,
                         ready=(split_ready, SPL["mem"]) if t == 0 else None)
                elif un[0] == "br":
                    unit(0, UIDX[un], 0, 0, 4, YH, YL, 4 * un[1], LB[o % 2], ready=(yl_ready, 4 * un[1]))
                else:
                    unit(0, UIDX[un], 0, 0, KB, XH, XL, 0, LB[o % 2],
                         ready=(split_ready, SPL["x"]) if un == ("xq", 0) else None)
                if t == 0:
                    norm("mem", TD[:, 0:M], M, SPL["mem"] + KB)
                if un == ("xq", 0):
                    norm("x", SS[:], S, SPL["x"] + KB)
            for e in EXTRA[t]:
                o = LEV[e]
                pe.wait_ge(lin_free, o + 1)
                if e[0] == "hn":
                    pe.wait_ge(h_sq, e[1] + 1)
                    last = mm(LB[o % 2][:], ONES[:], SQ[:], start=True, stop=True)
                elif e[1] == "gate":
                    pe.wait_ge(v_src, VSRC[e[1:]] + 1)
                    for k in range(TB):
                        last = nc.tensor.transpose(LB[o % 2][:, 64 * k:64 * k + 64], GT[:, 3, P * k:P * (k + 1)],
                                                   IDN[0:64, 0:64])
                else:
                    at64 = e[1] == "nav64"
                    pe.wait_ge(v_src, VSRC[("nav", e[2]) if at64 else e[1:]] + 1)
                    c0 = 64 if at64 else 0
                    for k in range({"memv": MB, "nav64": TB - 1}.get(e[1], TB)):
                        last = nc.tensor.transpose(LB[o % 2][:, P * k:P * (k + 1)],
                                                   TC[:, c0 + P * k:c0 + P * (k + 1)], IDN[:])
                last.then_inc(extra_full, 1)
            if st and st[0] in ("xa", "na"):
                for j in range(2):
                    pe.wait_ge(p_ready, 2 * g + j + 1)
                    if g >= 1:
                        pe.wait_ge(t_out, 2 * g + j - 1)
                    for k in range(MB):
                        last = nc.tensor.transpose(TRB[j][:, P * k:P * (k + 1)], SX[:, j, P * k:P * (k + 1)], IDN[:])
                    last.then_inc(t_full, 1)
        def branch(u0, o0, j, i, b):
            pe.wait_ge(lin_free, i * 12 + (o0 + j + 1))
            unit(u0, j, i, 12, 4, YH, YL, 4 * b, LB[(o0 + j) % 2],
                 ready=(mrg_lo, 0) if isinstance(i, int) and j == 0 else None)

        for j in range(4):
            branch(U["merge"], O["merge"], j, 0, (j + 2) % 3)
        with pe.Fori(1, 4) as i:
            for j in range(12):
                if j % 6 < 3:
                    pe.wait_ge(lin_free, i * 12 + (OM + j + 1))
                    unit(UM, j, i, 12, KB, XH, XL, 0, LB[(OM + j) % 2])
                else:
                    branch(UM, OM, j, i, j % 6 - 3)

        def linear(name, iters, per, xh, xl, ready, norm_of=None, before_last=None):
            def body(i, first):
                for j in range(per):
                    pe.wait_ge(lin_free, i * per + (O[name] + j + 1))
                    if first and j == 0:
                        unit(U[name], j, i, per, KB, xh, xl, 0, LB[O[name] % 2], ready=ready,
                             before_last=before_last)
                        if norm_of:
                            norm(norm_of, SS[:], S, SPL[norm_of] + KB)
                    else:
                        unit(U[name], j, i, per, KB, xh, xl, 0, LB[(O[name] + j) % 2])

            body(0, True)
            with pe.Fori(1, iters) as i:
                body(i, False)

        def down(name, l):
            with pe.Fori(0, 2) as i:
                for j in range(12):
                    if j % 3 == 0:
                        pe.wait_ge(lin_free, i * 4 + (O[name] + j // 3 + 1))
                    k0 = sum(DOWN_KC[:j % 3])
                    unit(U[name], j, i, 12, DOWN_KC[j % 3], FH, FL, k0, LB[(O[name] + j // 3) % 2],
                         start=j % 3 == 0, stop=j % 3 == 2, ready=(ffl_ready, FB * l + k0) if j < 3 else None)

        def after(name):
            return (split_ready, SPL[name])

        linear("out", 2, 4, GH, GL, (mrg_lo, 4))
        linear("up0", 11, 4, XH, XL, after("out"), "out")
        down("down0", 0)
        linear("ain", 2, 12, XH, XL, after("down0"), "down0")
        linear("aout", 2, 4, AH, AL, (al_ready, 0))
        linear("up1", 11, 4, XH, XL, after("aout"), "aout")
        down("down1", 1)
        pe.wait_ge(lin_free, O["f"] + 1)
        unit(U["f"], 0, 0, 0, KB, XH, XL, 0, LB[O["f"] % 2], ready=after("down1"))
        norm("down1", SS[:], S, SPL["down1"] + KB)

        def f_products(pp, s):
            g = 4 * pp + s
            for j in range(2):
                pe.wait_ge(ft_out, 2 * g + j + 1)
                if s == 0 and j == 0:
                    pe.wait_ge(f_v, pp + 1)
                    if pp:
                        pe.wait_ge(fo_free, pp)
                for k in range(s + 1):
                    last = mm(OB[0][64 * j:64 * j + 64, P * s:P * (s + 1)], FV[:, pp % 2, k, 64 * j:64 * j + 64],
                              FP[:, j, k * P:(k + 1) * P], start=k == 0, stop=k == s)
                last.then_inc(fpv, 1)

        for p in range(FA_PAIRS + 1):
            o0 = O["fa"] + FA_L * p
            for s in range(4):
                if p >= 1:
                    pp = p - 1
                    g = 4 * pp + s
                    nk = P * (s + 1)
                    if g == 0:
                        pe.wait_ge(mask_ready, 1)
                    if s == 0:
                        pe.wait_ge(f_epi, 2 * p)
                    for j in range(2):
                        if g >= 1:
                            pe.wait_ge(fs_read, 2 * g + j - 1)
                        r = slice(64 * j, 64 * j + 64)
                        mm(SB[j][:, 0:nk], FQ[r, pp % 2, P * s:P * (s + 1)], FK[r, pp % 2, 0:nk], start=True,
                           stop=False)
                        for h in range(2):
                            last = mm(SB[j][:, P * s + 64 * h:P * s + 64 * h + 64], NMR[r, h, :], IDR[r, r],
                                      start=False, stop=h == 1)
                        last.then_inc(fs_full, 1)
                if p < FA_PAIRS:
                    o = o0 + (0, 1, 3, 5)[s]
                    pe.wait_ge(lin_free, o + 1)
                    if s in (1, 2):
                        pe.wait_ge(q_sq, 2 * p + s)
                        mm(LB[o % 2][:], BLK[:], SQ[:], start=True, stop=True).then_inc(q_sum, 1)
                    if s == 3:
                        pe.wait_ge(f_src, p + 1)
                        for k in range(TB):
                            last = nc.tensor.transpose(LB[o % 2][:, P * k:P * (k + 1)], TC[:, P * k:P * (k + 1)],
                                                       IDN[:])
                        last.then_inc(f_trs, 1)
                    if s >= 1:
                        o += 1
                        pe.wait_ge(lin_free, o + 1)
                    xh, xl = ((XH, XL), (AH, AL), (XH, XL), (AH, AL))[s]
                    unit(U["fa"], 4 * p + s, 0, 0, KB, xh, xl, 0, LB[o % 2],
                         ready=(al_ready, KB) if p == 0 and s == 1 else None)
                if p >= 1:
                    if s >= 1:
                        f_products(pp, s - 1)
                    elif p >= 2:
                        f_products(pp - 1, 3)
                    for j in range(2):
                        pe.wait_ge(fp_ready, 2 * g + j + 1)
                        if g >= 1:
                            pe.wait_ge(ft_out, 2 * g + j - 1)
                        for k in range(s + 1):
                            last = nc.tensor.transpose(TRB[j][:, P * k:P * (k + 1)], FX[:, j, P * k:P * (k + 1)],
                                                       IDN[:])
                        last.then_inc(ft_full, 1)
        linear("bout", 2, 4, AH, AL, (ol_ready, 0), before_last=lambda: f_products(FA_PAIRS - 1, 3))
        linear("up2", 11, 4, XH, XL, after("bout"), "bout")
        down("down2", 2)

    block.__exit__(None, None, None)


def _units(w):
    k, n = w.shape
    return np.ascontiguousarray(w.reshape(k // P, P, n // P, P).transpose(2, 1, 0, 3).reshape(n // P, P, k))


def _cols(v):
    return np.asarray(v).reshape(-1, P).T


def kernel(**inp):
    import concourse.bacc as bacc
    from concourse.bass_utils import run_bass_kernel_spmd
    g = {k: np.asarray(v) for k, v in inp.items()}
    w_in = g["w_in"][0]
    c_ml, c_g, c_na, c_xa, c_mg = 0, 2048, 2064, 3600, 4112
    ml = [_units(w_in[:, c_ml + 512 * k:c_ml + 512 * (k + 1)]) for k in range(4)]
    na = [_units(w_in[:, c_na + 512 * k:c_na + 512 * (k + 1)]) for k in range(3)]
    xq = _units(w_in[:, c_xa:c_xa + 512])
    kv = _units(g["w_mem_kv"][0])
    wg = np.zeros((D, P), np.float32)
    gb = np.zeros((P,), np.float32)
    bi, bf = g["b_ml_igate"][0], g["b_ml_fgate"][0]
    for q, (src, b) in enumerate(((0, bi[0]), (2, bi[1]), (1, bf[0]), (3, bf[1]))):
        wg[:, 32 * q:32 * q + 4] = w_in[:, c_g + 4 * src:c_g + 4 * src + 4]
        gb[32 * q:32 * q + 4] = b
    of = {"memk": kv[0:4], "memv": kv[4:8], "xq": xq, "naq": na[0], "nak": na[1], "nav": na[2],
          "gate": _units(wg), "mlq": ml[0], "mlk": ml[1], "mlv": ml[2], "mlo": ml[3]}
    mg = _units(w_in[:, c_mg:])
    of["mg"] = [mg[(2 - q % 3) * 8 + q // 3] for q in range(6)]
    br = [_units(g[k][0]) for k in ("w_br_xa", "w_br_na", "w_br_ml")]
    of["br"] = [np.pad(br[b][0], ((0, 0), (0, UW // 2))) for b in range(2)]
    w_att = np.stack([of[k][n] for k, n in UNITS])
    w_mrg = np.stack([np.concatenate([mg[16 + n], mg[8 + n], mg[n], br[0][n], br[1][n], br[2][n]], axis=1)
                      for n in range(KB)])

    def pairs(w, parts):
        u = _units(w)
        n = len(u) // parts
        return np.ascontiguousarray(u.reshape(parts, n, P, -1).transpose(1, 0, 2, 3).reshape(parts * n, P, -1))

    wkvf, wqg = g["w_kvf_2"], g["b_w_qg_2"][0]
    uk, uv = _units(wkvf[:, 0:D]), _units(wkvf[:, D:2 * D])
    uq, ug = _units(wqg[:, 0:D]), _units(wqg[:, D:])
    w_fa = np.stack([x[p] for p in range(FA_PAIRS) for x in (uk, uq, uv, ug)])
    wf = np.zeros((D, P), np.float32)
    wf[:, 0:16] = wkvf[:, 2 * D:]
    bfc = np.zeros((P,), np.float32)
    bfc[0:16] = g["b_f_2"]
    pad = np.zeros((8, 2 * ROWS - 1, 2 * KC - 1), np.float32)
    pad[:, :, KC - 16:KC + 15] = g["na_rpb"][0]
    rpb = np.zeros((8, QC, ROWS, 3, KC, ROWS), np.float32)
    for c in range(QC):
        for r in range(ROWS):
            for v in range(3):
                x = KC - 1 - c - 8 * v
                rpb[:, c, r, v] = pad[:, ROWS - 1 - r:2 * ROWS - 1 - r, x:x + KC].transpose(0, 2, 1)
    rpb = rpb.reshape(NA_PAIRS, 2, P, 3, M).transpose(0, 2, 1, 3, 4)
    par = {"mix_g": g["mix_norm_g"][0], "mem_g": g["mem_norm_g"][0], "mlb": g["b_ml_conv"][0],
           "mlg": g["ml_norm_g"][0], "bmg": g["b_merge_gate"][0], "fg0": g["ffn_norm_g"][0],
           "fb0": g["b_ffn_conv"][0], "gb": gb, "ag0": g["attn_norm_2"][0], "ag1": g["attn_norm_2"][1],
           "fg1": g["ffn_norm_2"][0], "fg2": g["ffn_norm_2"][1], "kvg": g["kv_norm_2"], "bf": bfc,
           "kn": np.tile(g["k_norm_2"], 2), "qn": np.tile(g["q_norm_2"][0], 2)}
    par["fin"] = g["final_norm_g"]
    for k in range(3):
        par[f"mlc{k}"] = g["w_ml_conv"][0, k]
        par[f"fc0{k}"] = g["w_ffn_conv"][0, k]
        par[f"ac{k}"] = g["a_conv_2"][0, k]
        par[f"fc1{k}"] = g["ffn_conv_2"][0, k]
        par[f"fc2{k}"] = g["ffn_conv_2"][1, k]
    feat = lambda a: np.ascontiguousarray(a.T.reshape(KB, P, -1).transpose(1, 0, 2))
    arrays = {
        "x": feat(g["x"][0]), "mem": feat(g["mem"][0]),
        "par": np.ascontiguousarray(np.concatenate([_cols(par[n]) for n, _ in _COLS], axis=1)),
        "rpb": np.ascontiguousarray(rpb), "w_att": w_att, "w_mrg": w_mrg, "w_out": _units(g["w_out"][0]),
        "w_up0": pairs(g["w_ffn_up"][0], 2), "w_down0": _units(g["w_ffn_down"][0]),
        "w_ain": pairs(g["a_w_in_2"][0], 3), "w_aout": _units(g["a_w_out_2"][0]),
        "w_up1": pairs(g["ffn_w_up_2"][0], 2), "w_down1": _units(g["ffn_w_down_2"][0]),
        "w_f": _units(wf)[0], "w_fa": w_fa, "w_bout": _units(g["b_w_out_2"][0]),
        "w_up2": pairs(g["ffn_w_up_2"][1], 2), "w_down2": _units(g["ffn_w_down_2"][1]),
    }
    nc = bacc.Bacc("TRN2", target_bir_lowering=False, num_devices=1)
    aps = {k: nc.dram_tensor("in_" + k, a.shape, F32, kind="ExternalInput").ap() for k, a in arrays.items()}
    out = nc.dram_tensor("out_x", (KB, P, S), F32, kind="ExternalOutput").ap()
    two_blocks(nc, aps, out)
    r = run_bass_kernel_spmd(nc, [{"in_" + k: a for k, a in arrays.items()}], core_ids=[0])
    return np.ascontiguousarray(r.results[0]["out_x"].reshape(D, S).T)[None]
```
